# Optimizing a Trainium2 kernel written in Bass

```python
import math
import jax, jax.numpy as jnp
from jax import lax
import numpy as np

D_MODEL = 1024
BATCH = 1
SEQ = 2048
DEPTH = 1

CHUNK = 64
HEAD_DIM = 64
EPS = 1e-6
SWA_Q_HEADS = 8
SWA_KV_HEADS = 2
SWA_GROUP = SWA_Q_HEADS // SWA_KV_HEADS
WINDOW = 128
WINDOW_CHUNKS = WINDOW // CHUNK
SB_HEADS = 8
SB_BLOCK = 128
NUM_BUCKETS = 32
MAX_DISTANCE = 128
N_GROUPS = 4
EXPERTS_PER_GROUP = 8
N_EXPERTS = N_GROUPS * EXPERTS_PER_GROUP
TOP_K = 2
D_EXPERT = 512
ROW_BLOCK = 128
A_Q_WIDTH = SWA_Q_HEADS * HEAD_DIM
A_KV_WIDTH = SWA_KV_HEADS * HEAD_DIM
B_WIDTH = SB_HEADS * HEAD_DIM
N_BRANCH = 2
IN_WIDTHS = [A_Q_WIDTH, A_KV_WIDTH, A_KV_WIDTH, B_WIDTH, B_WIDTH, B_WIDTH, N_BRANCH * D_MODEL]
IN_WIDTH = sum(IN_WIDTHS)
IN_SPLITS = [int(v) for v in np.cumsum(IN_WIDTHS)[:-1]]

kernel_name = "hybrid_swa_stickbreak_hmoe_block"

def rms_norm(x, g):
    xf = x.astype(jnp.float32)
    y = xf * lax.rsqrt(jnp.mean(xf * xf, axis=-1, keepdims=True) + EPS)
    return (y * g.astype(jnp.float32)).astype(x.dtype)

def t5_bucket(rel):
    nb = NUM_BUCKETS // 2
    ret = jnp.where(rel > 0, nb, 0)
    n = jnp.abs(rel)
    max_exact = nb // 2
    nf = jnp.maximum(n, 1).astype(jnp.float32)
    large = max_exact + (jnp.log(nf / max_exact) / math.log(MAX_DISTANCE / max_exact)
                         * (nb - max_exact)).astype(jnp.int32)
    large = jnp.minimum(large, nb - 1)
    return ret + jnp.where(n < max_exact, n, large)

def band_rel_bias(table):
    qi = jnp.arange(CHUNK)[:, None]
    kj = jnp.arange(WINDOW)[None, :]
    rel = (kj - (WINDOW_CHUNKS - 1) * CHUNK) - qi
    bias = table[t5_bucket(rel)]
    return jnp.transpose(bias, (2, 0, 1)).reshape(SWA_KV_HEADS, SWA_GROUP, CHUNK, WINDOW)

def swa_sink_attention(q, k, v, g_q, g_k, sinks, rel_bias):
    B, S = q.shape[0], q.shape[1]
    nc = S // CHUNK
    q = rms_norm(q, g_q)
    k = rms_norm(k, g_k)
    qc = q.reshape(B, nc, CHUNK, SWA_KV_HEADS, SWA_GROUP, HEAD_DIM)
    kc = k.reshape(B, nc, CHUNK, SWA_KV_HEADS, HEAD_DIM)
    vc = v.reshape(B, nc, CHUNK, SWA_KV_HEADS, HEAD_DIM)

    def band(t):
        pieces = [jnp.pad(t, ((0, 0), (w, 0), (0, 0), (0, 0), (0, 0)))[:, :nc]
                  for w in range(WINDOW_CHUNKS - 1, 0, -1)]
        return jnp.concatenate(pieces + [t], axis=2)

    kb, vb = band(kc), band(vc)
    scores = jnp.einsum('bcqhgd,bcshd->bchgqs', qc, kb).astype(jnp.float32) * (HEAD_DIM ** -0.5)
    scores = scores + rel_bias.astype(jnp.float32)[None, None]
    chunk_of_slot = jnp.arange(nc)[:, None] - (WINDOW_CHUNKS - 1) + jnp.arange(WINDOW)[None, :] // CHUNK
    valid = (chunk_of_slot >= 0)[None, :, None, None, None, :]
    scores = jnp.where(valid, scores, -jnp.inf)
    sink = jnp.broadcast_to(sinks.astype(jnp.float32).reshape(1, 1, SWA_KV_HEADS, SWA_GROUP, 1, 1),
                            scores.shape[:-1] + (1,))
    probs = jax.nn.softmax(jnp.concatenate([scores, sink], axis=-1), axis=-1)[..., :WINDOW]
    out = jnp.einsum('bchgqs,bcshd->bcqhgd', probs.astype(v.dtype), vb)
    return out.reshape(B, S, SWA_Q_HEADS * HEAD_DIM)

def stick_breaking_attention(q, k, v):
    B, S, H, d = q.shape
    scale = HEAD_DIM ** -0.5
    outs = []
    for i in range(S // SB_BLOCK):
        lo, hi = i * SB_BLOCK, (i + 1) * SB_BLOCK
        z = jnp.einsum('bqhd,bkhd->bhqk', q[:, lo:hi], k[:, :hi]).astype(jnp.float32) * scale
        t = lo + jnp.arange(SB_BLOCK)[:, None]
        s = jnp.arange(hi)[None, :]
        causal = s < t
        log_keep = jnp.where(causal, jax.nn.log_sigmoid(-z), 0.0)
        after = lax.cumsum(log_keep, axis=3, reverse=True) - log_keep
        a = jnp.where(causal, jnp.exp(jax.nn.log_sigmoid(z) + after), 0.0)
        outs.append(jnp.einsum('bhqk,bkhd->bqhd', a.astype(v.dtype), v[:, :hi]))
    return jnp.concatenate(outs, axis=1).reshape(B, S, H * d)

def hierarchical_moe(h, w_group, b_group, w_router, b_router, w1, w3, w2):
    B, S, D = h.shape
    T = B * S
    xt = h.reshape(T, D)
    g_prob = jax.nn.softmax((xt @ w_group).astype(jnp.float32) + b_group.astype(jnp.float32), axis=-1)
    g_top, g_idx = lax.top_k(g_prob, 1)
    e_logits = ((xt @ w_router).astype(jnp.float32).reshape(T, N_GROUPS, EXPERTS_PER_GROUP)
                + b_router.astype(jnp.float32)[None])
    e_logits = jnp.take_along_axis(e_logits, g_idx[:, :, None], axis=1)[:, 0]
    e_top, e_idx = lax.top_k(jax.nn.softmax(e_logits, axis=-1), TOP_K)
    e_top = e_top / jnp.sum(e_top, axis=-1, keepdims=True)
    weights = (g_top * e_top).reshape(-1)
    eid = (g_idx * EXPERTS_PER_GROUP + e_idx).reshape(-1)
    tok = jnp.repeat(jnp.arange(T, dtype=jnp.int32), TOP_K)
    n_assign = T * TOP_K
    order = jnp.argsort(eid)
    s_eid, s_tok, s_w = eid[order], tok[order], weights[order]
    counts = jax.ops.segment_sum(jnp.ones_like(eid), eid, num_segments=N_EXPERTS)
    offsets = jnp.cumsum(counts) - counts
    padded = (counts + ROW_BLOCK - 1) // ROW_BLOCK * ROW_BLOCK
    pad_ends = jnp.cumsum(padded)
    pad_offsets = pad_ends - padded
    dest = pad_offsets[s_eid] + jnp.arange(n_assign) - offsets[s_eid]
    n_blocks = -(-n_assign // ROW_BLOCK) + N_EXPERTS
    n_rows = n_blocks * ROW_BLOCK
    row_tok = jnp.full((n_rows,), T, jnp.int32).at[dest].set(s_tok)
    row_w = jnp.zeros((n_rows,), jnp.float32).at[dest].set(s_w)
    block_start = jnp.arange(n_blocks) * ROW_BLOCK
    block_exp = jnp.minimum(jnp.sum(block_start[:, None] >= pad_ends[None, :], axis=1), N_EXPERTS - 1)
    x_pad = jnp.concatenate([xt, jnp.zeros((1, D), xt.dtype)], axis=0)
    xb = x_pad[row_tok].reshape(n_blocks, ROW_BLOCK, D)

    def expert_block(args):
        xr, e = args
        return (jax.nn.silu(xr @ w1[e]) * (xr @ w3[e])) @ w2[e]

    yb = lax.map(expert_block, (xb, block_exp)).reshape(n_rows, D)
    y = jax.ops.segment_sum(yb * row_w[:, None].astype(yb.dtype), row_tok, num_segments=T + 1)[:T]
    return y.reshape(B, S, D).astype(h.dtype)

def setup_inputs(seed: int = 0) -> dict:
    key = jax.random.key(seed)
    ks = jax.random.split(key, 20)
    f32 = jnp.float32
    nrm = lambda k, shape, scale: jax.random.normal(k, shape, f32) * scale
    return {
        "x": nrm(ks[0], (BATCH, SEQ, D_MODEL), 1.0),
        "norm_mix_g": 1.0 + nrm(ks[1], (DEPTH, D_MODEL), 0.02),
        "w_in": nrm(ks[2], (DEPTH, D_MODEL, IN_WIDTH), D_MODEL ** -0.5),
        "b_gate": nrm(ks[3], (DEPTH, N_BRANCH * D_MODEL), 0.02),
        "qa_norm_g": 1.0 + nrm(ks[4], (DEPTH, HEAD_DIM), 0.02),
        "ka_norm_g": 1.0 + nrm(ks[5], (DEPTH, HEAD_DIM), 0.02),
        "sinks": nrm(ks[6], (DEPTH, SWA_Q_HEADS), 0.5),
        "rel_bias_table": nrm(ks[7], (NUM_BUCKETS, SWA_Q_HEADS), 0.1),
        "w_proj_a": nrm(ks[8], (DEPTH, A_Q_WIDTH, D_MODEL), A_Q_WIDTH ** -0.5),
        "w_proj_b": nrm(ks[9], (DEPTH, B_WIDTH, D_MODEL), B_WIDTH ** -0.5),
        "w_out": nrm(ks[10], (DEPTH, D_MODEL, D_MODEL), D_MODEL ** -0.5),
        "norm_ffn_g": 1.0 + nrm(ks[11], (DEPTH, D_MODEL), 0.02),
        "w_group": nrm(ks[12], (DEPTH, D_MODEL, N_GROUPS), D_MODEL ** -0.5),
        "b_group": nrm(ks[13], (DEPTH, N_GROUPS), 0.01),
        "w_router": nrm(ks[14], (DEPTH, D_MODEL, N_EXPERTS), D_MODEL ** -0.5),
        "b_router": nrm(ks[15], (DEPTH, N_GROUPS, EXPERTS_PER_GROUP), 0.01),
        "w1": nrm(ks[16], (DEPTH, N_EXPERTS, D_MODEL, D_EXPERT), D_MODEL ** -0.5),
        "w3": nrm(ks[17], (DEPTH, N_EXPERTS, D_MODEL, D_EXPERT), D_MODEL ** -0.5),
        "w2": nrm(ks[18], (DEPTH, N_EXPERTS, D_EXPERT, D_MODEL), D_EXPERT ** -0.5),
    }

def reference(x, norm_mix_g, w_in, b_gate, qa_norm_g, ka_norm_g, sinks, rel_bias_table,
              w_proj_a, w_proj_b, w_out, norm_ffn_g, w_group, b_group, w_router, b_router,
              w1, w3, w2):
    B, S, D = x.shape
    rel_bias = band_rel_bias(rel_bias_table)
    for layer in range(DEPTH):
        h = rms_norm(x, norm_mix_g[layer])
        proj = h @ w_in[layer]
        qa, ka, va, qb, kb, vb, gates = jnp.split(proj, IN_SPLITS, axis=-1)
        ya = swa_sink_attention(qa.reshape(B, S, SWA_Q_HEADS, HEAD_DIM),
                                ka.reshape(B, S, SWA_KV_HEADS, HEAD_DIM),
                                va.reshape(B, S, SWA_KV_HEADS, HEAD_DIM),
                                qa_norm_g[layer], ka_norm_g[layer], sinks[layer], rel_bias)
        yb = stick_breaking_attention(qb.reshape(B, S, SB_HEADS, HEAD_DIM),
                                      kb.reshape(B, S, SB_HEADS, HEAD_DIM),
                                      vb.reshape(B, S, SB_HEADS, HEAD_DIM))
        gate = jax.nn.sigmoid((gates + b_gate[layer]).reshape(B, S, N_BRANCH, D))
        merged = gate[:, :, 0] * (ya @ w_proj_a[layer]) + gate[:, :, 1] * (yb @ w_proj_b[layer])
        x = x + (merged @ w_out[layer]).astype(x.dtype)
        h2 = rms_norm(x, norm_ffn_g[layer])
        x = x + hierarchical_moe(h2, w_group[layer], b_group[layer], w_router[layer], b_router[layer],
                                 w1[layer], w3[layer], w2[layer])
    return x


_drawn_inputs = setup_inputs


def setup_inputs(seed=0):
    import zlib

    import numpy as np

    out = dict(_drawn_inputs(seed))
    spreads = {}
    factors = {'b_gate': 5.142,
     'qa_norm_g': 8.0,
     'ka_norm_g': 7.195,
     'sinks': 8.0,
     'rel_bias_table': 3.117,
     'b_group': 14.067,
     'b_router': 4.218}
    for name, (base, spread) in spreads.items():
        noise = np.random.default_rng([zlib.crc32(name.encode()), seed]).standard_normal(out[name].shape)
        drawn = base * np.exp(spread * noise) if base else spread * noise
        out[name] = __import__('jax').numpy.asarray(drawn.astype(out[name].dtype))
    for name, factor in factors.items():
        out[name] = (out[name] * factor).astype(out[name].dtype)
    return out
```

```python
from contextlib import ExitStack

import numpy as np
import concourse.bass as bass
from concourse import mybir

F32 = mybir.dt.float32
F32R = mybir.dt.float32r
BF16 = mybir.dt.bfloat16
I32 = mybir.dt.int32
U32 = mybir.dt.uint32
ACT = mybir.ActivationFunctionType
ALU = mybir.AluOpType
AX = mybir.AxisListType

P = 128
D = 1024
S = 2048
KD = D // P
NT = S // P
TC = 512
NC_ = S // TC
CHUNK = 64
HD = 64
EPS = 1e-6
NF = 10
NQK = 8
NG = 16
SPAD = S + CHUNK
HB = 8
NE = 32
GR = 4
EG = NE // GR
F = 512
KF = F // P
MAXB = 2 * S // P + NE - 1
TRASH = S
OUT_ROWS = S + P


def passes3(nc, out, w_hi, w_lo, x_hi, x_lo, first, last):
    nc.tensor.matmul(out, w_hi, x_hi, start=first, stop=False)
    nc.tensor.matmul(out, w_hi, x_lo, start=False, stop=False)
    return nc.tensor.matmul(out, w_lo, x_hi, start=False, stop=last)


class Chain:

    def __init__(self, eng, sem, base=0):
        self.eng, self.sem, self.base, self.n = eng, sem, base, 0

    def __call__(self, ins):
        self.n += 1
        ins.then_inc(self.sem, 1)
        self.eng.wait_ge(self.sem, self.base + self.n)


def norm_transpose(nc, x, g, ident_d, hT_hi, hT_lo):
    with ExitStack() as c:
        sb = lambda n, s, d=F32: c.enter_context(nc.sbuf_tensor(n, s, d))
        sem = lambda n: c.enter_context(nc.semaphore(n))
        xt = sb("nt_x", [P, 2, D])
        h = sb("nt_h", [P, 2, D])
        junk = sb("nt_sq", [P, D])
        g_bc = sb("nt_g", [P, D])
        ident = sb("nt_ident", [P, P])
        ssq = sb("nt_ssq", [P, 2])
        rms = sb("nt_rms", [P, 2])
        eps = sb("nt_eps", [P, 1])
        rstd = sb("nt_rstd", [P, 2])
        pt = c.enter_context(nc.psum_tensor("nt_ps", [P, 2, KD, P], F32))
        const_in = sem("nt_const_in")
        x_in = [sem("nt_x_in0"), sem("nt_x_in1")]
        x_free = sem("nt_x_free")
        sq_done = sem("nt_sq_done")
        eps_set = sem("nt_eps_set")
        rms_ready = sem("nt_rms_ready")
        rstd_ready = sem("nt_rstd_ready")
        h_ready = sem("nt_h_ready")
        transposed = sem("nt_transposed")
        hi_done = sem("nt_hi_done")
        ps_free = sem("nt_ps_free")
        G = 4
        block = c.enter_context(nc.Block())

        @block.sync
        def _(sp):
            sp.dma_start(g_bc[:, :], g.partition_broadcast(P)).then_inc(const_in, 16)
            sp.dma_start(ident[:, :], ident_d).then_inc(const_in, 16)
            with sp.Fori(0, NT // G) as i:
                for u in range(G):
                    sp.wait_ge(x_free, i * G + u + 1)
                    sp.dma_start(xt[:, u % 2, :], x[bass.ds(i * (G * P) + u * P, P), :]) \
                        .then_inc(x_in[u % 2], 16)

        @block.gpsimd
        def _(pool):
            nc.gpsimd.memset(eps[:, :], EPS).then_inc(eps_set, 1)

        @block.scalar
        def _(act):
            act.wait_ge(eps_set, 1)

            def square(i, u):
                act.wait_ge(x_in[u % 2], (i * (G // 2) + u // 2 + 1) * 16)
                nc.scalar.activation(junk[:, :], xt[:, u % 2, :], ACT.Square,
                                     accum_out=ssq[:, u % 2:u % 2 + 1]).then_inc(sq_done, 1)
                act.wait_ge(sq_done, i * G + u + 1)
                nc.scalar.activation(rms[:, u % 2:u % 2 + 1], ssq[:, u % 2:u % 2 + 1], ACT.Sqrt,
                                     scale=1.0 / D, bias=eps[:, :]).then_inc(rms_ready, 1)

            def take_hi(i, u):
                act.wait_ge(transposed, i * G + u + 3)
                nc.scalar.copy(hT_hi[:, :, bass.ds(i * (G * P) + u * P, P)], pt[:, u % 2, :, :]) \
                    .then_inc(hi_done, 1)

            with act.Fori(0, NT // G) as i:
                square(i, 0)
                square(i, 1)
                for u in range(G):
                    take_hi(i, u)
                    if u + 2 < G:
                        square(i, u + 2)

        @block.vector
        def _(dve):
            nc.vector.sem_inc(x_free, 2)
            nc.vector.sem_inc(ps_free, 2)
            dve.wait_ge(const_in, 32)

            def normalise(i, u):
                v = u % 2
                dve.wait_ge(rms_ready, i * G + u + 1)
                nc.vector.reciprocal(rstd[:, v:v + 1], rms[:, v:v + 1]).then_inc(rstd_ready, 1)
                dve.wait_ge(rstd_ready, i * G + u + 1)
                dve.wait_ge(transposed, i * G + u + 1)
                nc.vector.scalar_tensor_tensor(h[:, v, :], xt[:, v, :], rstd[:, v:v + 1], g_bc[:, :],
                                               ALU.mult, ALU.mult).then_inc(h_ready, 1)
                dve.wait_ge(h_ready, i * G + u + 1)
                nc.vector.sem_inc(x_free, 1)

            def take_lo(i, u):
                dve.wait_ge(hi_done, i * G + u + 1)
                sl = bass.ds(i * (G * P) + u * P, P)
                nc.vector.tensor_tensor(hT_lo[:, :, sl], pt[:, u % 2, :, :], hT_hi[:, :, sl],
                                        ALU.subtract).then_inc(ps_free, 1)

            with dve.Fori(0, NT // G) as i:
                normalise(i, 0)
                normalise(i, 1)
                for u in range(G):
                    take_lo(i, u)
                    if u + 2 < G:
                        normalise(i, u + 2)

        @block.tensor
        def _(pe):
            nc.tensor.sem_inc(transposed, 2)
            pe.wait_ge(const_in, 32)
            with pe.Fori(0, NT // G) as i:
                for u in range(G):
                    pe.wait_ge(h_ready, i * G + u + 1)
                    pe.wait_ge(ps_free, i * G + u + 1)
                    for k in range(KD):
                        last = nc.tensor.transpose(pt[:, u % 2, k, :], h[:, u % 2, k * P:(k + 1) * P],
                                                   ident[:, :])
                    last.then_inc(transposed, 1)


def input_projection(nc, w_tiles, b_gate, hT_hi, hT_lo, projF, qk_hi, qk_lo, gates):
    with ExitStack() as c:
        sb = lambda n, s, d=F32: c.enter_context(nc.sbuf_tensor(n, s, d))
        sem = lambda n: c.enter_context(nc.semaphore(n))
        w = sb("ip_w", [P, 2, KD, P])
        w_hi = sb("ip_w_hi", [P, 2, KD, P], F32R)
        w_lo = sb("ip_w_lo", [P, 2, KD, P], F32R)
        o = sb("ip_out", [P, 2, S])
        o_hi = o[:, :, :].bitcast(F32R)
        o_lo = sb("ip_out_lo", [P, 2, S], F32R)
        bias = sb("ip_bias", [P, NG])
        zero = sb("ip_zero", [P, CHUNK])
        ps = c.enter_context(nc.psum_tensor("ip_ps", [P, 2, S], F32))
        w_in = [sem("ip_w_in0"), sem("ip_w_in1")]
        w_split = sem("ip_w_split")
        hi_done = sem("ip_w_hi_done")
        mm_done = sem("ip_mm_done")
        read_out = sem("ip_read_out")
        out_hi = sem("ip_out_hi")
        stored = [sem("ip_stored0"), sem("ip_stored1")]
        bias_in = sem("ip_bias_in")
        zero_set = sem("ip_zero_set")
        pads = sem("ip_pads")
        block = c.enter_context(nc.Block())
        NTL = NF + NQK + NG
        LAST = NTL // 2 - 1
        PARTS = [(0, NF // 2, "f32"), (NF // 2, (NF + NQK) // 2, "split"),
                 ((NF + NQK) // 2, LAST, "gate")]

        @block.sync
        def _(sp):
            sp.dma_start(bias[:, :], b_gate).then_inc(bias_in, 16)
            with sp.Fori(0, NTL // 2) as i:
                for u in range(2):
                    sp.wait_ge(w_split, i * 2 + u + 1)
                    sp.dma_start(w[:, u, :, :], w_tiles[bass.ds(i * 2 + u, 1), :, :, :]
                                 .rearrange("a p k c -> p (a k) c")).then_inc(w_in[u], 16)

        @block.gpsimd
        def _(pool):
            nc.gpsimd.memset(zero[:, :], 0.0).then_inc(zero_set, 1)
            pool.wait_ge(zero_set, 1)
            for t in (4, 5):
                pool.dma_start(projF[t, :, S:SPAD], zero[:, :]).then_inc(pads, 16)
            pool.wait_ge(pads, 32)

        @block.vector
        def _(dve):
            nc.vector.sem_inc(w_split, 2)

            def split_weight(n, u):
                dve.wait_ge(w_in[u], n * 8 - u * 8 + 16)
                dve.wait_ge(hi_done, n + 1)
                nc.vector.tensor_tensor(w_lo[:, u, :, :], w[:, u, :, :], w_hi[:, u, :, :],
                                        ALU.subtract).then_inc(w_split, 1)

            def read_lo(n, u):
                dve.wait_ge(out_hi, n - NF + 1)
                nc.vector.tensor_tensor(o_lo[:, u, :], ps[:, u, :], o_hi[:, u, :],
                                        ALU.subtract).then_inc(read_out, 1)

            split_weight(0, 0)
            split_weight(1, 1)
            for first, end, kind in PARTS:
                with dve.Fori(first, end) as i:
                    for u in range(2):
                        split_weight(i * 2 + u + 2, u)
                        if kind == "split":
                            read_lo(i * 2 + u, u)

        @block.scalar
        def _(act):
            nc.scalar.sem_inc(read_out, 2)
            act.wait_ge(bias_in, 16)

            def round_weight(n, u):
                act.wait_ge(w_in[u], n * 8 - u * 8 + 16)
                act.wait_ge(mm_done, n + 1)
                nc.scalar.copy(w_hi[:, u, :, :], w[:, u, :, :]).then_inc(hi_done, 1)

            def read(kind, i, u):
                n = i * 2 + u
                act.wait_ge(mm_done, n + 3)
                if kind == "f32":
                    done = i * 16 + 16
                elif kind == "split":
                    done = i * 32 + (16 - NF // 2 * 16)
                else:
                    done = i * 16 + (16 + NQK // 2 * 16)
                act.wait_ge(stored[u], done)
                src = ps[:, u, :]
                if kind == "f32":
                    nc.scalar.copy(o[:, u, :], src).then_inc(read_out, 1)
                    act.wait_ge(read_out, n + 3)
                    act.dma_start(projF[bass.ds(n, 1), :, 0:S].rearrange("a p s -> p (a s)"), o[:, u, :]) \
                        .then_inc(stored[u], 16)
                elif kind == "gate":
                    nc.scalar.activation(o[:, u, :], src, ACT.Sigmoid,
                                         bias=bias[:, bass.ds(n - (NF + NQK), 1)]).then_inc(read_out, 1)
                    act.wait_ge(read_out, n + 3)
                    act.dma_start(gates[bass.ds(n - (NF + NQK), 1), :, :].rearrange("a p s -> p (a s)"),
                                  o[:, u, :]).then_inc(stored[u], 16)
                else:
                    nc.scalar.copy(o_hi[:, u, :], src).then_inc(out_hi, 1)
                    act.wait_ge(read_out, n + 3)
                    for dst, part in ((qk_hi, o), (qk_lo, o_lo[:, :, :].bitcast(F32))):
                        act.dma_start(dst[bass.ds(n - NF, 1), :, :].rearrange("a p s -> p (a s)"),
                                      part[:, u, :]).then_inc(stored[u], 16)

            nc.scalar.sem_inc(stored[0], 16)
            nc.scalar.sem_inc(stored[1], 16)
            round_weight(0, 0)
            round_weight(1, 1)
            for first, end, kind in PARTS:
                with act.Fori(first, end) as i:
                    for u in range(2):
                        round_weight(i * 2 + u + 2, u)
                        read(kind, i, u)
            for u in range(2):
                read("gate", LAST, u)
            for u in range(2):
                act.wait_ge(stored[u], 16 + (NTL + NQK) // 2 * 16)

        @block.tensor
        def _(pe):
            nc.tensor.sem_inc(mm_done, 2)
            with pe.Fori(0, NTL // 2) as i:
                for u in range(2):
                    pe.wait_ge(w_split, i * 2 + u + 3)
                    pe.wait_ge(read_out, i * 2 + u + 1)
                    for t in range(NC_):
                        cols = slice(t * TC, (t + 1) * TC)
                        for k in range(KD):
                            last = passes3(nc, ps[:, u, cols], w_hi[:, u, k, :], w_lo[:, u, k, :],
                                           hT_hi[:, k, cols], hT_lo[:, k, cols], k == 0, k == KD - 1)
                    last.then_inc(mm_done, 1)


def band_bias(nc, table, onehot, bias_d):
    with ExitStack() as c:
        sb = lambda n, s, d=F32: c.enter_context(nc.sbuf_tensor(n, s, d))
        sem = lambda n: c.enter_context(nc.semaphore(n))
        NB = 32
        tab = sb("bb_tab", [NB, 8])
        oh = sb("bb_onehot", [NB, CHUNK * P])
        line = sb("bb_line", [8, CHUNK * P])
        ps = c.enter_context(nc.psum_tensor("bb_ps", [P, 2, TC], F32))
        loaded, mm, read, stored = sem("bb_loaded"), sem("bb_mm"), sem("bb_read"), sem("bb_stored")
        block = c.enter_context(nc.Block())
        n_mm = CHUNK * P // TC

        @block.sync
        def _(sp):
            sp.dma_start(tab[:, :], table).then_inc(loaded, 16)
            sp.dma_start(oh[:, :], onehot).then_inc(loaded, 16)
            sp.wait_ge(read, n_mm)
            sp.dma_start(bias_d.rearrange("h i j -> h (i j)"), line[:, :]).then_inc(stored, 16)
            sp.wait_ge(stored, 16)

        @block.tensor
        def _(pe):
            pe.wait_ge(loaded, 32)
            for m in range(n_mm):
                if m >= 2:
                    pe.wait_ge(read, m - 1)
                nc.tensor.matmul(ps[0:8, m % 2, :], tab[:, :], oh[:, m * TC:(m + 1) * TC],
                                 start=True, stop=True).then_inc(mm, 1)

        @block.vector
        def _(dve):
            for m in range(n_mm):
                dve.wait_ge(mm, m + 1)
                nc.vector.tensor_copy(line[:, m * TC:(m + 1) * TC], ps[0:8, m % 2, :]).then_inc(read, 1)


def banded_attention(nc, projF, g_q, g_k, sinks, bias_d, ident_d, pair_ones, yaT):
    with ExitStack() as c:
        sb = lambda n, s, d=F32: c.enter_context(nc.sbuf_tensor(n, s, d))
        sem = lambda n: c.enter_context(nc.semaphore(n))
        KW = P + CHUNK
        q = sb("ba_q", [P, 2, 4, P])
        k = sb("ba_k", [P, 2, KW])
        v = sb("ba_v", [P, 2, KW])
        qsq = sb("ba_qsq", [P, 4, P])
        ksq = sb("ba_ksq", [P, KW])
        rq = sb("ba_rq", [P, 4, P])
        rk = sb("ba_rk", [P, KW])
        lnq = sb("ba_lnq", [P, 4, P])
        lnk = sb("ba_lnk", [P, KW])
        qn = sb("ba_qn", [P, 2, 4, CHUNK])
        kn = sb("ba_kn", [P, KW])
        vn = sb("ba_vn", [P, 2, 2, P])
        s = sb("ba_s", [P, 2, 2, 4, P])
        e = sb("ba_e", [P, 8, P])
        pT = sb("ba_pT", [P, 2, 4 * P])
        o = sb("ba_o", [P, 2, 4, 2, CHUNK])
        bias = sb("ba_bias", [P, 4, P])
        bias_end = sb("ba_bias_end", [P, 4, P])
        sink = sb("ba_sink", [P, 2, 4])
        gq, gk = sb("ba_gq", [P, 1]), sb("ba_gk", [P, 1])
        eps = sb("ba_eps", [P, 1])
        ident, ones = sb("ba_ident", [P, P]), sb("ba_ones", [P, P])
        mx, negm, sneg = sb("ba_mx", [P, 8]), sb("ba_negm", [P, 8]), sb("ba_sneg", [P, 8])
        esink, rowsum = sb("ba_esink", [P, 8]), sb("ba_rowsum", [P, 8])
        den, rden = sb("ba_den", [P, 8]), sb("ba_rden", [P, 8])
        pb = lambda n, sh: c.enter_context(nc.psum_tensor(n, sh, F32))
        ps_q, ps_k = pb("ba_ps_q", [P, 4, P]), pb("ba_ps_k", [P, TC])
        ps_v = pb("ba_ps_v", [P, 4, P])
        ps_s = pb("ba_ps_s", [P, 2, 2, 2, P])
        ps_t = pb("ba_ps_t", [P, 2, 4 * P])
        ps_o = pb("ba_ps_o", [P, 2, 4 * CHUNK])
        const_in, prep = sem("ba_const_in"), sem("ba_prep")
        loaded = [sem("ba_loaded0"), sem("ba_loaded1")]
        squared, ssq_done = sem("ba_squared"), sem("ba_ssq_done")
        act_step, dve_step = sem("ba_act_step"), sem("ba_dve_step")
        r_ready, qk_ready = sem("ba_r_ready"), sem("ba_qk_ready")
        v_turned, vn_ready = sem("ba_v_turned"), sem("ba_vn_ready")
        scored, s_ready = sem("ba_scored"), sem("ba_s_ready")
        max_ready, exp_done, p_ready = sem("ba_max_ready"), sem("ba_exp_done"), sem("ba_p_ready")
        p_turned, pT_ready = sem("ba_p_turned"), sem("ba_pT_ready")
        pv_done, o_ready = sem("ba_pv_done"), sem("ba_o_ready")
        stored = [sem("ba_stored0"), sem("ba_stored1")]
        block = c.enter_context(nc.Block())
        N = NT
        PAIRS = N // 2 - 1

        @block.sync
        def _(sp):
            for h2 in range(2):
                half = slice(h2 * CHUNK, (h2 + 1) * CHUNK)
                sp.dma_start(bias[half, :, :], bias_d.rearrange("(a b) i j -> b i a j", b=2)[h2]) \
                    .then_inc(const_in, 16)
                sp.dma_start(sink[half, 0, :], sinks[h2, :]
                             .partition_broadcast(CHUNK)).then_inc(const_in, 16)
                sp.dma_start(gq[half, :], g_q).then_inc(const_in, 16)
                sp.dma_start(gk[half, :], g_k).then_inc(const_in, 16)
            sp.dma_start(ident[:, :], ident_d).then_inc(const_in, 16)
            sp.dma_start(ones[:, :], pair_ones).then_inc(const_in, 16)

            with sp.Fori(0, N // 2) as i:
                for u in range(2):
                    sp.wait_ge(o_ready, i * 2 + u + 2)
                    sp.dma_start(yaT[:, :, bass.ds(i * (2 * P) + u * P, P)].rearrange("t p s -> p t s"),
                                   o[:, u, :, :, :].rearrange("p t c s -> p t (c s)")) \
                        .then_inc(stored[u], 16)
            for u in range(2):
                sp.wait_ge(stored[u], 16 + N // 2 * 16)

        @block.gpsimd
        def _(pool):
            def load(n, u):
                pool.dma_start(q[:, u, :, :], projF[0:4, :, bass.ds(n * P, P)].rearrange("t p s -> p t s")) \
                    .then_inc(loaded[u], 16)
                pool.dma_start(k[:, u, :], projF[4, :, bass.ds(n * P, KW)]).then_inc(loaded[u], 16)
                pool.dma_start(v[:, u, :], projF[5, :, bass.ds(n * P, KW)]).then_inc(loaded[u], 16)

            load(0, 0)
            load(1, 1)
            with pool.Fori(1, N // 2) as i:
                for u in range(2):
                    pool.wait_ge(qk_ready, i * 2 + u - 1)
                    pool.wait_ge(v_turned, i * 2 + u - 1)
                    load(i * 2 + u, u)

        @block.scalar
        def _(act):
            act.wait_ge(const_in, 160)
            act.wait_ge(prep, 2)

            def squares(n, u):
                act.wait_ge(loaded[u], n * 24 - u * 24 + 48)
                if not (isinstance(n, int) and n == 0):
                    act.wait_ge(ssq_done, n)
                nc.scalar.activation(qsq[:, :, :], q[:, u, :, :], ACT.Square).then_inc(act_step, 1)
                nc.scalar.activation(ksq[:, :], k[:, u, :], ACT.Square).then_inc(squared, 1)
                act.wait_ge(act_step, n * 4 + 1)

            def rstd(n, u):
                act.wait_ge(ssq_done, n + 1)
                nc.scalar.activation(lnq[:, :, :], ps_q[:, :, :], ACT.Ln, scale=1.0 / HD,
                                     bias=eps[:, :]).then_inc(act_step, 1)
                nc.scalar.activation(lnk[:, :], ps_k[:, 0:KW], ACT.Ln, scale=1.0 / HD,
                                     bias=eps[:, :]).then_inc(act_step, 1)
                act.wait_ge(act_step, n * 4 + 3)
                if not (isinstance(n, int) and n == 0):
                    act.wait_ge(qk_ready, n)
                nc.scalar.activation(rq[:, :, :], lnq[:, :, :], ACT.Exp, scale=-0.5).then_inc(act_step, 1)
                nc.scalar.activation(rk[:, :], lnk[:, :], ACT.Exp, scale=-0.5).then_inc(r_ready, 1)
                act.wait_ge(act_step, n * 4 + 4)

            def take_v(n, u):
                act.wait_ge(v_turned, n + 1)
                if not (isinstance(n, int) and n == 0):
                    act.wait_ge(pv_done, n)
                nc.scalar.copy(vn[:, u, :, :], ps_v[:, 0:2, :]).then_inc(vn_ready, 1)

            def exps(n, u):
                act.wait_ge(max_ready, n + 1)
                for a in range(8):
                    nc.scalar.activation(e[:, a, :], s[:, u, a // 4, a % 4, :], ACT.Exp,
                                         bias=negm[:, a:a + 1], accum_out=rowsum[:, a:a + 1])
                nc.scalar.activation(esink[:, :], sneg[:, :], ACT.Exp).then_inc(exp_done, 1)

            def take_pT(n, u):
                for cc in range(2):
                    act.wait_ge(p_turned, n * 2 + cc + 1)
                    nc.scalar.copy(pT[:, cc, :], ps_t[:, cc, :]).then_inc(pT_ready, 1)

            def step(n, u, front):
                if front:
                    squares(n + 1, 1 - u)
                exps(n, u)
                if front:
                    rstd(n + 1, 1 - u)
                    take_v(n + 1, 1 - u)
                take_pT(n, u)

            nc.scalar.sem_inc(pT_ready, 2)
            squares(0, 0)
            rstd(0, 0)
            take_v(0, 0)
            with act.Fori(0, PAIRS) as i:
                for u in range(2):
                    step(i * 2 + u, u, True)
            step(N - 2, 0, True)
            step(N - 1, 1, False)

        @block.vector
        def _(dve):
            nc.vector.memset(eps[:, :], EPS).then_inc(prep, 1)
            dve.wait_ge(const_in, 160)
            chain = Chain(dve, dve_step)
            chain(nc.vector.tensor_copy(bias_end[:, :, :], bias[:, :, :]))
            chain(nc.vector.memset(bias_end[:, :, CHUNK:P], -1.0e30))
            nc.vector.tensor_copy(sink[:, 1, :], sink[:, 0, :]).then_inc(prep, 1)
            dve.wait_ge(prep, 2)
            STEPS = 6

            def norms(n, u):
                dve.wait_ge(r_ready, n + 1)
                if not (isinstance(n, int) and n == 0):
                    dve.wait_ge(scored, n)
                for cc in range(2):
                    own = slice(cc * CHUNK, (cc + 1) * CHUNK)
                    nc.vector.scalar_tensor_tensor(qn[:, cc, :, :], q[:, u, :, own], gq[:, :],
                                                   rq[:, :, own], ALU.mult, ALU.mult)
                nc.vector.scalar_tensor_tensor(kn[:, :], k[:, u, :], gk[:, :], rk[:, :],
                                               ALU.mult, ALU.mult).then_inc(qk_ready, 1)

            def take_scores(n, u, last=False):
                dve.wait_ge(scored, n + 1)
                for g in range(2):
                    for cc in range(2):
                        b = bias_end if last and cc else bias
                        ins = nc.vector.scalar_tensor_tensor(
                            s[:, u, cc, 2 * g:2 * g + 2, :], ps_s[:, g, cc, :, :], HD ** -0.5,
                            b[:, 2 * g:2 * g + 2, :], ALU.mult, ALU.add)
                ins.then_inc(s_ready, 1)

            def maxima(n, u, chain):
                dve.wait_ge(s_ready, n + 1)
                chain(nc.vector.tensor_reduce(mx[:, :], s[:, u, :, :, :].rearrange("p c t s -> p (c t) s"),
                                              AX.X, ALU.max))
                chain(nc.vector.tensor_tensor(mx[:, :], mx[:, :], sink[:, :, :].rearrange("p c t -> p (c t)"),
                                              ALU.max))
                chain(nc.vector.tensor_scalar(negm[:, :], mx[:, :], -1.0, None, ALU.mult))
                nc.vector.tensor_tensor(sneg[:, :], negm[:, :], sink[:, :, :].rearrange("p c t -> p (c t)"),
                                        ALU.add).then_inc(max_ready, 1)

            def probs(n, u, chain):
                dve.wait_ge(exp_done, n + 1)
                chain(nc.vector.tensor_tensor(den[:, :], rowsum[:, :], esink[:, :], ALU.add))
                chain(nc.vector.reciprocal(rden[:, :], den[:, :]))
                nc.vector.tensor_tensor(e[:, :, :], e[:, :, :],
                                        rden[:, :].unsqueeze(2).to_broadcast([P, 8, P]), ALU.mult) \
                    .then_inc(p_ready, 1)

            def take_o(n, u):
                dve.wait_ge(pv_done, n + 2)
                dve.wait_ge(stored[u], n * 8 - u * 8 + 16)
                nc.vector.tensor_copy(o[:, u, :, :, :].rearrange("p t c s -> p c t s"),
                                      ps_o[:, :, :].rearrange("p c (t s) -> p c t s", t=4)) \
                    .then_inc(o_ready, 1)

            def step(n, u, front, last=False):
                chain = Chain(dve, dve_step, n * (STEPS - 1) + 2)
                maxima(n, u, chain)
                probs(n, u, chain)
                if front:
                    norms(n + 1, 1 - u)
                    take_scores(n + 1, 1 - u, last)
                take_o(n, u)

            norms(0, 0)
            take_scores(0, 0)
            nc.vector.sem_inc(stored[0], 16)
            nc.vector.sem_inc(stored[1], 16)
            nc.vector.sem_inc(o_ready, 1)
            with dve.Fori(0, PAIRS) as i:
                for u in range(2):
                    step(i * 2 + u, u, True)
            step(N - 2, 0, True, last=True)
            step(N - 1, 1, False)

        @block.tensor
        def _(pe):
            nc.tensor.sem_inc(pv_done, 1)
            pe.wait_ge(const_in, 160)

            def front1(n, u):
                pe.wait_ge(squared, n + 1)
                if not (isinstance(n, int) and n == 0):
                    pe.wait_ge(r_ready, n)
                    pe.wait_ge(vn_ready, n)
                nc.tensor.matmul(ps_q[:, :, :], ones[:, :], qsq[:, :, :], start=True, stop=True)
                nc.tensor.matmul(ps_k[:, 0:KW], ones[:, :], ksq[:, :], start=True, stop=True) \
                    .then_inc(ssq_done, 1)
                for cc in range(2):
                    last = nc.tensor.transpose(ps_v[:, cc, :], v[:, u, cc * CHUNK:cc * CHUNK + P], ident[:, :])
                last.then_inc(v_turned, 1)

            def front2(n, u):
                pe.wait_ge(qk_ready, n + 1)
                if not (isinstance(n, int) and n == 0):
                    pe.wait_ge(s_ready, n)
                for cc in range(2):
                    for pr in range(2):
                        for g in range(2):
                            rows = slice(g * HD, (g + 1) * HD)
                            last = nc.tensor.matmul(ps_s[:, g, cc, pr, :],
                                                    qn[rows, cc, 2 * pr:2 * pr + 2, :]
                                                    .rearrange("p t s -> p (t s)"),
                                                    kn[rows, cc * CHUNK:cc * CHUNK + P], start=True, stop=True)
                last.then_inc(scored, 1)

            def turn_p(n, u):
                pe.wait_ge(p_ready, n + 1)
                for cc in range(2):
                    pe.wait_ge(pT_ready, n * 2 + cc + 1)
                    for a in range(4):
                        last = nc.tensor.transpose(ps_t[:, cc, a * P:(a + 1) * P], e[:, cc * 4 + a, :], ident[:, :])
                    last.then_inc(p_turned, 1)

            def products(n, u):
                pe.wait_ge(vn_ready, n + 1)
                pe.wait_ge(o_ready, n + 1)
                for cc in range(2):
                    pe.wait_ge(pT_ready, n * 2 + cc + 3)
                    for g in range(2):
                        last = nc.tensor.matmul(ps_o[g * HD:(g + 1) * HD, cc, :], vn[:, u, cc, g * HD:(g + 1) * HD],
                                                pT[:, cc, g * 2 * P:(g + 1) * 2 * P], start=True, stop=True)
                last.then_inc(pv_done, 1)

            def step(n, u, front):
                if front:
                    front1(n + 1, 1 - u)
                turn_p(n, u)
                if front:
                    front2(n + 1, 1 - u)
                products(n, u)

            front1(0, 0)
            front2(0, 0)
            with pe.Fori(0, PAIRS) as i:
                for u in range(2):
                    step(i * 2 + u, u, True)
            step(N - 2, 0, True)
            step(N - 1, 1, False)


def stick_breaking(nc, projF, qk_hi, qk_lo, ident_d, neg_ident, mask_d, ybT):
    UNITS = [(t, off, min(TC, S - P * t - off)) for t in range(NT) for off in range(0, S - P * t, TC)]
    NU = len(UNITS)
    BODY = [(u, t, off, w) for u in range(2) for t, off, w in UNITS]
    NBODY = 2 * NU
    CR = 4
    ends = [j for j, (_, t, off, w) in enumerate(BODY) if t % 4 == 3 and P * t + off + w == S]
    last_unit = {(u, t): j for j, (u, t, _, _) in enumerate(BODY)}
    by_act = [j % 5 == 2 for j in range(NBODY)]
    with ExitStack() as c:
        sb = lambda n, s, d=F32: c.enter_context(nc.sbuf_tensor(n, s, d))
        sem = lambda n: c.enter_context(nc.semaphore(n))
        qs = sb("sb_q", [P, 2, S], F32R)
        kh = sb("sb_kh", [P, 2, S], F32R)
        kl = sb("sb_kl", [P, 2, S], F32R)
        vT = sb("sb_vT", [P, S])
        v = sb("sb_v", [P, NT, P])
        sig = sb("sb_sig", [P, 4, TC])
        R = sb("sb_R", [P, 2, S + 1])
        aT = sb("sb_aT", [P, 2, TC])
        y = sb("sb_y", [HD, 2, TC])
        zeros = sb("sb_zeros", [P, TC])
        ident = sb("sb_ident", [P, P])
        nident, mask = sb("sb_nident", [P, P], BF16), sb("sb_mask", [P, P], BF16)
        stage = sb("sb_stage", [P, 2, P])
        z = c.enter_context(nc.psum_tensor("sb_z", [P, 3, TC], F32))
        ps_t = c.enter_context(nc.psum_tensor("sb_pst", [P, 2, TC], F32))
        ps_v = c.enter_context(nc.psum_tensor("sb_psv", [P, TC], F32))
        ps_y = c.enter_context(nc.psum_tensor("sb_psy", [P, 2, TC], F32))
        const_in, prep = sem("sb_const_in"), sem("sb_prep")
        head_in = [sem("sb_head_in0"), sem("sb_head_in1")]
        v_in = sem("sb_v_in")
        v_turned, v_ready = sem("sb_v_turned"), sem("sb_v_ready")
        z_done, sig_done, scan_done = sem("sb_z_done"), sem("sb_sig_done"), sem("sb_scan_done")
        a_done, t_done = sem("sb_a_done"), sem("sb_t_done")
        aT_act, aT_dve = sem("sb_aT_act"), sem("sb_aT_dve")
        y_done, y_read = sem("sb_y_done"), sem("sb_y_read")
        stored = [sem("sb_stored0"), sem("sb_stored1")]
        block = c.enter_context(nc.Block())
        ROUNDS = HB // 2

        def unit(eng, s, i, j):
            eng.wait_ge(s, i * NBODY + (CR + j + 1))

        @block.sync
        def _(sp):
            sp.dma_start(ident[:, :], ident_d).then_inc(const_in, 16)
            sp.dma_start(stage[:, 0, :], neg_ident).then_inc(const_in, 16)
            sp.dma_start(stage[:, 1, :], mask_d).then_inc(const_in, 16)
            sp.sem_inc(stored[0], 16)
            sp.sem_inc(stored[1], 16)

            def load_v(i):
                sp.dma_start(vT[:, :], projF[bass.ds(i + 6, 1), :, 0:S].rearrange("a p s -> p (a s)")) \
                    .then_inc(v_in, 16)

            def store(i, m):
                sp.wait_ge(y_read, i * 8 + (m + 1 + CR))
                u, g = divmod(m, 4)
                sp.dma_start(ybT[bass.ds(i, 1), u * HD:(u + 1) * HD, g * TC:(g + 1) * TC]
                             .rearrange("a p s -> p (a s)"), y[:, m % 2, :]).then_inc(stored[m % 2], 16)

            load_v(0)
            with sp.Fori(0, ROUNDS - 1) as i:
                for m in range(8):
                    store(i, m)
                    if m == 3:
                        load_v(i + 1)
            for m in range(8):
                store(ROUNDS - 1, m)
            for b in range(2):
                sp.wait_ge(stored[b], 16 + ROUNDS * 4 * 16)

        @block.scalar
        def _(act):
            for s in (sig_done,):
                nc.scalar.sem_inc(s, CR)
            nc.scalar.sem_inc(y_read, CR)

            def sigmoids(i, j):
                _, t, off, w = BODY[j]
                unit(act, z_done, i, j)
                unit(act, t_done, i, j - 4)
                nc.scalar.activation(sig[:, j % 4, 0:w], z[:, j % 3, 0:w], ACT.Sigmoid, scale=HD ** -0.5)
                nc.scalar.activation(z[:, j % 3, 0:w], z[:, j % 3, 0:w], ACT.Sigmoid, scale=-HD ** -0.5) \
                    .then_inc(sig_done, 1)

            def take_v(i, b):
                act.wait_ge(v_turned, i * 4 + (b + 1))
                nc.scalar.copy(v[:, 4 * b:4 * b + 4, :].rearrange("p t d -> p (t d)"), ps_v[:, :]) \
                    .then_inc(v_ready, 1)

            def take_y(i, m):
                act.wait_ge(y_done, i * 8 + (m + 1))
                act.wait_ge(stored[m % 2], i * 64 + (m // 2 * 16 + 16))
                nc.scalar.copy(y[:, m % 2, :], ps_y[0:HD, m % 2, :]).then_inc(y_read, 1)

            with act.Fori(0, ROUNDS) as i:
                for j in range(NBODY + 7):
                    if j < 4:
                        take_v(i, j)
                    if j < NBODY:
                        sigmoids(i, j)
                    if 0 <= j - 3 < NBODY and by_act[j - 3]:
                        w = BODY[j - 3][3]
                        unit(act, t_done, i, j - 3)
                        nc.scalar.copy(aT[:, (j - 3) % 2, 0:w], ps_t[:, (j - 3) % 2, 0:w]).then_inc(aT_act, 1)
                    if j - 6 in ends:
                        take_y(i, ends.index(j - 6))

        @block.vector
        def _(dve):
            nc.vector.sem_inc(scan_done, CR)
            nc.vector.memset(zeros[:, :], 0.0)
            nc.vector.memset(R[:, :, 0:1], 1.0).then_inc(prep, 1)
            dve.wait_ge(const_in, 48)
            nc.vector.tensor_copy(nident[:, :], stage[:, 0, :])
            nc.vector.tensor_copy(mask[:, :], stage[:, 1, :]).then_inc(prep, 1)
            dve.wait_ge(prep, 2)

            def scan(i, j):
                u, t, off, w = BODY[j]
                unit(dve, sig_done, i, j)
                if off:
                    unit(dve, scan_done, i, j - 1)
                    first = R[:, t % 2, off:off + 1]
                else:
                    first = 1.0
                    before = last_unit[(u, t - 2)] if t >= 2 else last_unit[(1 - u, NT - 2 + t)] - (0 if u else NBODY)
                    unit(dve, a_done, i, before)
                nc.vector.tensor_tensor_scan(R[:, t % 2, off + 1:off + w + 1], z[:, j % 3, 0:w],
                                             zeros[:, 0:w], first, ALU.mult, ALU.max).then_inc(scan_done, 1)

            with dve.Fori(0, ROUNDS) as i:
                for j in range(NBODY + 2):
                    if j < NBODY:
                        scan(i, j)
                    if 0 <= j - 2 < NBODY and not by_act[j - 2]:
                        w = BODY[j - 2][3]
                        unit(dve, t_done, i, j - 2)
                        nc.vector.tensor_copy(aT[:, (j - 2) % 2, 0:w], ps_t[:, (j - 2) % 2, 0:w]) \
                            .then_inc(aT_dve, 1)

        @block.gpsimd
        def _(pool):
            nc.gpsimd.sem_inc(a_done, CR)

            def load_head(i, u):
                half = slice(u * HD, (u + 1) * HD)
                for dst, rows, src, t in (
                        (qs, 0, qk_hi, 0), (qs, HD, qk_lo, 0), (kh, 0, qk_hi, 4), (kh, HD, qk_hi, 4),
                        (kl, 0, qk_lo, 4), (kl, HD, qk_lo, 4)):
                    pool.dma_start(dst[rows:rows + HD, u, :],
                                   src[bass.ds(i + t, 1), half, :].rearrange("a p s -> p (a s)")) \
                        .then_inc(head_in[u], 16)

            load_head(0, 0)
            load_head(0, 1)

            def weights(i, more):
                for j in range(NBODY):
                    _, t, off, w = BODY[j]
                    unit(pool, scan_done, i, j)
                    nc.gpsimd.tensor_tensor(sig[:, j % 4, 0:w], sig[:, j % 4, 0:w],
                                            R[:, t % 2, off:off + w], ALU.mult).then_inc(a_done, 1)
                    if more and (j == NBODY - 1 or BODY[j + 1][0] != BODY[j][0]):
                        load_head(i + 1, BODY[j][0])

            with pool.Fori(0, ROUNDS - 1) as i:
                weights(i, True)
            weights(ROUNDS - 1, False)

        @block.tensor
        def _(pe):
            nc.tensor.sem_inc(z_done, CR)
            nc.tensor.sem_inc(t_done, CR)
            pe.wait_ge(prep, 2)

            def turn_v(i, b):
                if b == 0:
                    pe.wait_ge(v_in, i * 16 + 16)
                else:
                    pe.wait_ge(v_ready, i * 4 + b)
                for t in range(4):
                    last = nc.tensor.transpose(ps_v[:, t * P:(t + 1) * P],
                                               vT[:, (b * 4 + t) * P:(b * 4 + t + 1) * P], ident[:, :])
                last.then_inc(v_turned, 1)

            def scores(i, j):
                u, t, off, w = BODY[j]
                if t == 0 and off == 0:
                    pe.wait_ge(head_in[u], i * 96 + 96)
                unit(pe, scan_done, i, j - 3)
                cols = slice(P * t + off, P * t + off + w)
                q_t = qs[:, u, P * t:P * (t + 1)]
                nc.tensor.matmul(z[:, j % 3, 0:w], q_t, kh[:, u, cols], start=True, stop=False)
                if off == 0:
                    nc.tensor.matmul(z[:, j % 3, 0:P], nident[:, :], mask[:, :], start=False, stop=False)
                nc.tensor.matmul(z[:, j % 3, 0:w], q_t, kl[:, u, cols], start=False, stop=True) \
                    .then_inc(z_done, 1)

            def turn_a(i, j):
                w = BODY[j][3]
                unit(pe, a_done, i, j)
                for b in range(w // P):
                    last = nc.tensor.transpose(ps_t[:, j % 2, b * P:(b + 1) * P],
                                               sig[:, j % 4, b * P:(b + 1) * P], ident[:, :])
                last.then_inc(t_done, 1)

            def product(i, j):
                u, t, off, w = BODY[j]
                if by_act[j]:
                    pe.wait_ge(aT_act, i * sum(by_act) + sum(by_act[:j + 1]))
                else:
                    pe.wait_ge(aT_dve, i * (NBODY - sum(by_act)) + (j + 1 - sum(by_act[:j + 1])))
                group = u * 4 + t // 4
                if off == 0:
                    pe.wait_ge(y_read, i * 8 + (group - 1 + CR))
                if j < 4:
                    pe.wait_ge(v_ready, i * 4 + (j + 1))
                for b in range(w // P):
                    kt = t + off // P + b
                    last = nc.tensor.matmul(ps_y[0:HD, group % 2, (t % 4) * P:(t % 4 + 1) * P],
                                            v[:, kt, u * HD:(u + 1) * HD], aT[:, j % 2, b * P:(b + 1) * P],
                                            start=kt == t, stop=kt == NT - 1)
                if j in ends:
                    last.then_inc(y_done, 1)

            with pe.Fori(0, ROUNDS) as i:
                for j in range(NBODY + 4):
                    if j < 4:
                        turn_v(i, j)
                    if j < NBODY:
                        scores(i, j)
                    if 0 <= j - 3 < NBODY:
                        turn_a(i, j - 3)
                    if j >= 4:
                        product(i, j - 4)


def merge_branches(nc, yaT, ybT, gates, wp_tiles, mT_hi_d, mT_lo_d):
    with ExitStack() as c:
        sb = lambda n, s, d=F32: c.enter_context(nc.sbuf_tensor(n, s, d))
        sem = lambda n: c.enter_context(nc.semaphore(n))
        y_hi = sb("mb_y_hi", [P, 8, S], F32R)
        y_lo = sb("mb_y_lo", [P, 8, S], F32R)
        y = sb("mb_y", [P, 2, 4, TC])
        w = sb("mb_w", [P, 2, KD, P])
        w_hi, w_lo = sb("mb_w_hi", [P, 2, KD, P], F32R), sb("mb_w_lo", [P, 2, KD, P], F32R)
        ga, gb = sb("mb_ga", [P, S]), sb("mb_gb", [P, S])
        ta, tb = sb("mb_ta", [P, TC]), sb("mb_tb", [P, TC])
        m = sb("mb_m", [P, TC])
        m_hi, m_lo = sb("mb_m_hi", [P, 2, TC], F32R), sb("mb_m_lo", [P, 2, TC], F32R)
        ps = c.enter_context(nc.psum_tensor("mb_ps", [P, 4, 2, TC], F32))
        y_in = [sem("mb_y_in0"), sem("mb_y_in1")]
        y_rounded, y_split = sem("mb_y_rounded"), sem("mb_y_split")
        w_in = [sem("mb_w_in0"), sem("mb_w_in1")]
        w_rounded, w_split = sem("mb_w_rounded"), sem("mb_w_split")
        g_in = sem("mb_g_in")
        mm_done = sem("mb_mm_done")
        read_out = sem("mb_read_out")
        dve_step, m_ready = sem("mb_dve_step"), sem("mb_m_ready")
        m_rounded, m_split = sem("mb_m_rounded"), sem("mb_m_split")
        stored = [sem("mb_stored0"), sem("mb_stored1")]
        block = c.enter_context(nc.Block())
        NO = D // P

        @block.gpsimd
        def _(pool):
            for t in range(NC_):
                cols = slice(t * TC, (t + 1) * TC)
                for br, src in enumerate((yaT, ybT)):
                    if t:
                        pool.wait_ge(y_split, 2 * t + br - 1)
                    pool.dma_start(y[:, br, :, :], src[:, :, cols].rearrange("t p s -> p t s")).then_inc(y_in[br], 16)

            def load_gates(n):
                pool.dma_start(ga[:, :], gates[bass.ds(n, 1), :, :].rearrange("a p s -> p (a s)")).then_inc(g_in, 16)
                pool.dma_start(gb[:, :], gates[bass.ds(n + 8, 1), :, :].rearrange("a p s -> p (a s)")).then_inc(g_in, 16)

            load_gates(0)
            with pool.Fori(1, NO) as n:
                pool.wait_ge(read_out, n * NC_ + 4)
                load_gates(n)

        @block.sync
        def _(sp):
            sp.sem_inc(stored[0], 32)
            sp.sem_inc(stored[1], 32)

            def load_w(n, u):
                sp.dma_start(w[:, u, :, :], wp_tiles[bass.ds(n, 1), :, :, :]
                             .rearrange("a p k c -> p (a k) c")).then_inc(w_in[u], 16)

            def store(n, u):
                for t in range(NC_):
                    sp.wait_ge(m_split, n * NC_ + t + 1)
                    for dst, src in ((mT_hi_d, m_hi), (mT_lo_d, m_lo)):
                        sp.dma_start(dst[bass.ds(n, 1), :, t * TC:(t + 1) * TC].rearrange("a p s -> p (a s)"),
                                     src[:, t % 2, :].bitcast(F32)).then_inc(stored[t % 2], 16)

            load_w(0, 0)
            load_w(1, 1)
            with sp.Fori(0, NO // 2 - 1) as i:
                for u in range(2):
                    sp.wait_ge(w_split, i * 2 + u + 3)
                    load_w(i * 2 + u + 2, u)
                    store(i * 2 + u, u)
            for u in range(2):
                store(NO - 2 + u, u)
            for b in range(2):
                sp.wait_ge(stored[b], 32 + NO * NC_ // 2 * 32)

        @block.scalar
        def _(act):
            nc.scalar.sem_inc(w_rounded, 2)

            def round_weight(n, u):
                act.wait_ge(w_in[u], n * 8 - u * 8 + 16)
                act.wait_ge(mm_done, n * NC_ + NC_)
                nc.scalar.copy(w_hi[:, u, :, :], w[:, u, :, :]).then_inc(w_rounded, 1)

            def round_m(n):
                for t in range(NC_):
                    act.wait_ge(m_ready, n * NC_ + t + 1)
                    act.wait_ge(stored[t % 2], n * 64 + t // 2 * 32 + 32)
                    nc.scalar.copy(m_hi[:, t % 2, :], m[:, :]).then_inc(m_rounded, 1)

            round_weight(0, 0)
            round_weight(1, 1)
            for t in range(NC_):
                for br in range(2):
                    act.wait_ge(y_in[br], 16 * (t + 1))
                    nc.scalar.copy(y_hi[:, br * 4:br * 4 + 4, t * TC:(t + 1) * TC], y[:, br, :, :]) \
                        .then_inc(y_rounded, 1)
            with act.Fori(0, NO // 2 - 1) as i:
                for u in range(2):
                    round_m(i * 2 + u)
                    round_weight(i * 2 + u + 2, u)
            for u in range(2):
                round_m(NO - 2 + u)

        @block.vector
        def _(dve):
            nc.vector.sem_inc(w_split, 2)
            nc.vector.sem_inc(read_out, 4)

            def split_weight(n, u):
                dve.wait_ge(w_rounded, n + 3)
                nc.vector.tensor_tensor(w_lo[:, u, :, :], w[:, u, :, :], w_hi[:, u, :, :],
                                        ALU.subtract).then_inc(w_split, 1)

            def gate_chunks(n):
                dve.wait_ge(g_in, n * 32 + 32)
                for t in range(NC_):
                    cols = slice(t * TC, (t + 1) * TC)
                    dve.wait_ge(mm_done, n * NC_ + t + 9)
                    nc.vector.tensor_tensor(ta[:, :], ps[:, t, 0, :], ga[:, cols], ALU.mult).then_inc(dve_step, 1)
                    nc.vector.tensor_tensor(tb[:, :], ps[:, t, 1, :], gb[:, cols], ALU.mult).then_inc(read_out, 1)
                    dve.wait_ge(dve_step, n * NC_ + t + 1)
                    dve.wait_ge(read_out, n * NC_ + t + 5)
                    nc.vector.tensor_tensor(m[:, :], ta[:, :], tb[:, :], ALU.add).then_inc(m_ready, 1)
                    dve.wait_ge(m_rounded, n * NC_ + t + 1)
                    nc.vector.tensor_tensor(m_lo[:, t % 2, :], m[:, :], m_hi[:, t % 2, :],
                                            ALU.subtract).then_inc(m_split, 1)

            split_weight(0, 0)
            split_weight(1, 1)
            for t in range(NC_):
                for br in range(2):
                    dve.wait_ge(y_rounded, 2 * t + br + 1)
                    part = (slice(None), slice(br * 4, br * 4 + 4), slice(t * TC, (t + 1) * TC))
                    nc.vector.tensor_tensor(y_lo[part], y[:, br, :, :], y_hi[part], ALU.subtract).then_inc(y_split, 1)
            with dve.Fori(0, NO // 2 - 1) as i:
                for u in range(2):
                    gate_chunks(i * 2 + u)
                    split_weight(i * 2 + u + 2, u)
            for u in range(2):
                gate_chunks(NO - 2 + u)

        @block.tensor
        def _(pe):
            nc.tensor.sem_inc(mm_done, 8)

            def tile(n, u, wait_y=False):
                pe.wait_ge(w_split, n + 3)
                for t in range(NC_):
                    cols = slice(t * TC, (t + 1) * TC)
                    if wait_y:
                        pe.wait_ge(y_split, 2 * t + 2)
                    pe.wait_ge(read_out, n * NC_ + t + 1)
                    for br in range(2):
                        for k in range(4):
                            kk = br * 4 + k
                            last = passes3(nc, ps[:, t, br, :], w_hi[:, u, kk, :], w_lo[:, u, kk, :],
                                           y_hi[:, kk, cols], y_lo[:, kk, cols], k == 0, k == 3)
                    last.then_inc(mm_done, 1)

            tile(0, 0, True)
            tile(1, 1)
            with pe.Fori(1, NO // 2) as i:
                for u in range(2):
                    tile(i * 2 + u, u)


def output_projection(nc, mT_hi_d, mT_lo_d, wo_d, x, g2, wr_d, ident_d, h2_d, out, logits):
    with ExitStack() as c:
        sb = lambda n, s, d=F32: c.enter_context(nc.sbuf_tensor(n, s, d))
        sem = lambda n: c.enter_context(nc.semaphore(n))
        NR = GR + NE
        wo = sb("op_wo", [P, KD, D])
        wo_hi, wo_lo = sb("op_wo_hi", [P, KD, D], F32R), sb("op_wo_lo", [P, KD, D], F32R)
        m_hi, m_lo = sb("op_m_hi", [P, 2, KD, P], F32R), sb("op_m_lo", [P, 2, KD, P], F32R)
        xt, x1 = sb("op_x", [P, 2, D]), sb("op_x1", [P, 2, D])
        h2, junk = sb("op_h2", [P, 2, D]), sb("op_sq", [P, D])
        h2T = sb("op_h2T", [P, KD, P])
        g_bc, ident = sb("op_g", [P, D]), sb("op_ident", [P, P])
        wr = sb("op_wr", [P, KD, NR])
        eps, ssq = sb("op_eps", [P, 1]), sb("op_ssq", [P, 1])
        rms, rstd = sb("op_rms", [P, 1]), sb("op_rstd", [P, 1])
        ps = c.enter_context(nc.psum_tensor("op_ps", [P, 2, D], F32))
        ps_t = c.enter_context(nc.psum_tensor("op_ps_t", [P, KD, P], F32))
        ps_l = c.enter_context(nc.psum_tensor("op_ps_l", [P, TC], F32))
        const_in = sem("op_const_in")
        wo_in = [sem(f"op_wo_in{k}") for k in range(KD)]
        wo_rounded, wo_split, prep = sem("op_wo_rounded"), sem("op_wo_split"), sem("op_prep")
        tile_in = [sem("op_tile_in0"), sem("op_tile_in1")]
        mm_done, x1_done = sem("op_mm_done"), sem("op_x1_done")
        sq_done, rms_ready, rstd_ready = sem("op_sq_done"), sem("op_rms_ready"), sem("op_rstd_ready")
        h2_ready, turned, h2T_ready = sem("op_h2_ready"), sem("op_turned"), sem("op_h2T_ready")
        l_done, l_read = sem("op_l_done"), sem("op_l_read")
        stored = [sem("op_stored0"), sem("op_stored1")]
        block = c.enter_context(nc.Block())

        @block.gpsimd
        def _(pool):
            nc.gpsimd.memset(eps[:, :], EPS).then_inc(prep, 1)
            def load(n, u):
                cols = bass.ds(n * P, P)
                for dst, src in ((m_hi, mT_hi_d), (m_lo, mT_lo_d)):
                    pool.dma_start(dst[:, u, :, :], src[:, :, cols].rearrange("k p s -> p k s")).then_inc(tile_in[u], 16)
                pool.dma_start(xt[:, u, :], x[cols, :]).then_inc(tile_in[u], 16)

            load(0, 0)
            load(1, 1)
            with pool.Fori(1, NT // 2) as i:
                for u in range(2):
                    pool.wait_ge(x1_done, i * 2 + u + 1)
                    load(i * 2 + u, u)

        @block.sync
        def _(sp):
            for k in range(KD):
                sp.dma_start(wo[:, k, :], wo_d[:, k, :]).then_inc(wo_in[k], 16)
            sp.dma_start(g_bc[:, :], g2.partition_broadcast(P)).then_inc(const_in, 16)
            sp.dma_start(ident[:, :], ident_d).then_inc(const_in, 16)
            sp.dma_start(wr[:, :, :], wr_d).then_inc(const_in, 16)
            sp.sem_inc(stored[0], 32)
            sp.sem_inc(stored[1], 32)
            with sp.Fori(0, NT // 2) as i:
                for u in range(2):
                    rows = bass.ds(i * (2 * P) + u * P, P)
                    sp.wait_ge(x1_done, i * 2 + u + 3)
                    sp.dma_start(out[rows, :], x1[:, u, :]).then_inc(stored[u], 16)
                    sp.wait_ge(h2_ready, i * 2 + u + 1)
                    sp.dma_start(h2_d[rows, :], h2[:, u, :]).then_inc(stored[u], 16)
            sp.dma_start(out[TRASH:OUT_ROWS, :], h2[:, 1, :]).then_inc(stored[1], 16)
            sp.dma_start(h2_d[TRASH:OUT_ROWS, :], h2[:, 1, :]).then_inc(stored[1], 16)
            sp.wait_ge(stored[0], 32 + NT // 2 * 32)
            sp.wait_ge(stored[1], 64 + NT // 2 * 32)

        @block.scalar
        def _(act):
            for k in range(KD):
                act.wait_ge(wo_in[k], 16)
                nc.scalar.copy(wo_hi[:, k, :], wo[:, k, :]).then_inc(wo_rounded, 1)
            act.wait_ge(prep, 1)
            with act.Fori(0, NT) as n:
                act.wait_ge(x1_done, n + 3)
                nc.scalar.activation(junk[:, :], x1[:, bass.ds(n % 2, 1), :]
                                     .rearrange("p a s -> p (a s)"), ACT.Square, accum_out=ssq[:, :]).then_inc(sq_done, 1)
                act.wait_ge(sq_done, n + 1)
                nc.scalar.activation(rms[:, :], ssq[:, :], ACT.Sqrt, scale=1.0 / D, bias=eps[:, :]) \
                    .then_inc(rms_ready, 1)
                act.wait_ge(turned, n + 1)
                nc.scalar.copy(h2T[:, :, :], ps_t[:, :, :]).then_inc(h2T_ready, 1)

        @block.vector
        def _(dve):
            nc.vector.sem_inc(x1_done, 2)
            for k in range(KD):
                dve.wait_ge(wo_rounded, k + 1)
                nc.vector.tensor_tensor(wo_lo[:, k, :], wo[:, k, :], wo_hi[:, k, :],
                                        ALU.subtract).then_inc(wo_split, 1)
            dve.wait_ge(const_in, 48)
            with dve.Fori(0, NT // 2) as i:
                for u in range(2):
                    n = i * 2 + u
                    dve.wait_ge(mm_done, n + 1)
                    dve.wait_ge(stored[u], i * 32 + 32)
                    nc.vector.tensor_tensor(x1[:, u, :], ps[:, u, :], xt[:, u, :], ALU.add).then_inc(x1_done, 1)
                    dve.wait_ge(rms_ready, n + 1)
                    nc.vector.reciprocal(rstd[:, :], rms[:, :]).then_inc(rstd_ready, 1)
                    dve.wait_ge(rstd_ready, n + 1)
                    nc.vector.scalar_tensor_tensor(h2[:, u, :], x1[:, u, :], rstd[:, :], g_bc[:, :],
                                                   ALU.mult, ALU.mult).then_inc(h2_ready, 1)
                    dve.wait_ge(l_done, n + 1)
                    nc.vector.tensor_copy(logits[:, bass.ds(n, 1), :].rearrange("p a e -> p (a e)"),
                                          ps_l[:, 0:NR]).then_inc(l_read, 1)

        @block.tensor
        def _(pe):
            pe.wait_ge(wo_split, KD)
            pe.wait_ge(const_in, 48)

            def half(n, u, hf):
                if hf == 0:
                    pe.wait_ge(tile_in[u], n * 24 - u * 24 + 48)
                    pe.wait_ge(x1_done, n + 1)
                cols = slice(hf * TC, (hf + 1) * TC)
                for k in range(KD):
                    last = passes3(nc, ps[:, u, cols], m_hi[:, u, k, :],
                                   m_lo[:, u, k, :], wo_hi[:, k, cols],
                                   wo_lo[:, k, cols], k == 0, k == KD - 1)
                if hf:
                    last.then_inc(mm_done, 1)

            def turn(n, u):
                pe.wait_ge(h2_ready, n + 1)
                for k in range(KD):
                    last = nc.tensor.transpose(ps_t[:, k, :], h2[:, u, k * P:(k + 1) * P], ident[:, :])
                last.then_inc(turned, 1)

            def route(n):
                pe.wait_ge(h2T_ready, n + 1)
                if not (isinstance(n, int) and n == 0):
                    pe.wait_ge(l_read, n)
                for k in range(KD):
                    last = nc.tensor.matmul(ps_l[:, 0:NR], h2T[:, k, :], wr[:, k, :], start=k == 0, stop=k == KD - 1)
                last.then_inc(l_done, 1)

            def step(n, u):
                half(n, u, 0)
                turn(n - 1, 1 - u)
                half(n, u, 1)
                route(n - 1)

            half(0, 0, 0)
            half(0, 0, 1)
            step(1, 1)
            with pe.Fori(1, NT // 2) as i:
                for u in range(2):
                    step(i * 2 + u, u)
            turn(NT - 1, 1)
            route(NT - 1)


C_IOTA, C_REV4, C_REV8, C_THR, C_TOK, C_TRI, C_ONES, C_TRASH = 0, 128, 132, 140, 156, 172, 300, 428
CW = 429
BT = 66


def routing(nc, logits, bias_all, cst_d, idx_all, w_all, blk_exp, last_pair):
    with ExitStack() as c:
        sb = lambda n, s, d=F32: c.enter_context(nc.sbuf_tensor(n, s, d))
        sem = lambda n: c.enter_context(nc.semaphore(n))
        NR = GR + NE
        cst = sb("rt_cst", [P, CW])
        b_bc = sb("rt_bias", [P, NR])
        lg = sb("rt_lg", [P, NT, NR])
        gm, gk = sb("rt_gm", [P, NT]), sb("rt_gk", [P, NT])
        gs, key4, ohg = sb("rt_gs", [P, NT, GR]), sb("rt_key4", [P, NT, GR]), sb("rt_ohg", [P, NT, GR])
        gsum, gtop = sb("rt_gsum", [P, NT]), sb("rt_gtop", [P, NT])
        sel, es = sb("rt_sel", [P, NT, GR, EG]), sb("rt_es", [P, NT, EG])
        es2, key8 = sb("rt_es2", [P, NT, EG]), sb("rt_key8", [P, NT, EG])
        oh = [sb("rt_oh0", [P, NT, EG]), sb("rt_oh1", [P, NT, EG])]
        mx = [sb("rt_mx0", [P, NT]), sb("rt_mx1", [P, NT])]
        OH = [sb("rt_OH0", [P, NT, GR, EG]), sb("rt_OH1", [P, NT, GR, EG])]
        O = sb("rt_O", [P, NT, NE])
        acc = sb("rt_acc", [P, NT + 1, NE])
        ed, sd = sb("rt_ed", [P, NT]), sb("rt_sd", [P, NT])
        w = sb("rt_w", [P, 2, NT])
        cmp_, nblk = sb("rt_cmp", [P, NE, NT]), sb("rt_nblk", [P, NE])
        ends, off = sb("rt_ends", [P, NE]), sb("rt_off", [P, NE])
        dest, dsel = sb("rt_dest", [P, NT, NE]), sb("rt_dsel", [P, NT, NE])
        d = sb("rt_d", [P, 2, NT])
        di, hi_i, lo_i = sb("rt_di", [P, 32], I32), sb("rt_hi_i", [P, 32], I32), sb("rt_lo_i", [P, 32], I32)
        hi, lo = sb("rt_hi", [P, 32]), sb("rt_lo", [P, 32])
        row1h = sb("rt_row1h", [P, 2, P])
        blk1h = sb("rt_blk1h", [P, 2, 3, 64])
        tab = sb("rt_tab", [P, 3, 64])
        tmp = sb("rt_tmp", [P, 64])
        bcmp, bsum = sb("rt_bcmp", [1, 64, NE]), sb("rt_bsum", [1, 64])
        npf, npi = sb("rt_npf", [1, 1]), sb("rt_npi", [1, 1], I32)
        ps_r = c.enter_context(nc.psum_tensor("rt_ps_r", [P, NT, NE], F32))
        ps_c = c.enter_context(nc.psum_tensor("rt_ps_c", [P, TC], F32))
        ps_b = c.enter_context(nc.psum_tensor("rt_ps_b", [P, TC], F32))
        const_in, step = sem("rt_const_in"), sem("rt_step")
        exp_in, exp_out = sem("rt_exp_in"), sem("rt_exp_out")
        O_ready, ranks = sem("rt_O_ready"), sem("rt_ranks")
        hot_ready, hot_used = sem("rt_hot_ready"), sem("rt_hot_used")
        block = c.enter_context(nc.Block())
        iota = cst[:, C_IOTA:C_IOTA + P]
        bc = lambda ap, shape: ap.to_broadcast(shape)

        @block.sync
        def _(sp):
            sp.dma_start(cst[:, :], cst_d).then_inc(const_in, 16)
            sp.dma_start(b_bc[:, :], bias_all.partition_broadcast(P)).then_inc(const_in, 16)

        @block.scalar
        def _(act):
            act.wait_ge(exp_in, 1)
            nc.scalar.activation(gs[:, :, :], gs[:, :, :], ACT.Exp).then_inc(exp_out, 1)
            act.wait_ge(exp_in, 2)
            nc.scalar.activation(ed[:, :], ed[:, :], ACT.Exp).then_inc(exp_out, 1)

        @block.tensor
        def _(pe):
            pe.wait_ge(const_in, 32)
            pe.wait_ge(O_ready, 1)
            tri, ones = cst[:, C_TRI:C_TRI + P], cst[:, C_ONES:C_ONES + P]
            nc.tensor.matmul(ps_r[:, :, :], tri, O[:, :, :], start=True, stop=False)
            nc.tensor.matmul(ps_r[:, :, :], ones, acc[:, 0:NT, :], start=False, stop=True)
            nc.tensor.matmul(ps_c[:, 0:NE], ones, acc[:, NT, :], start=True, stop=True).then_inc(ranks, 1)
            for a in range(32):
                pe.wait_ge(hot_ready, a + 1)
                nc.tensor.matmul(ps_b[:, 0:192], row1h[:, a % 2, :],
                                 blk1h[:, a % 2, :, :].rearrange("p c b -> p (c b)"),
                                 start=a == 0, stop=a == 31).then_inc(hot_used, 1)

        @block.vector
        def _(dve):
            V = nc.vector
            ch = Chain(dve, step)
            dve.wait_ge(const_in, 32)
            ch(V.tensor_tensor(lg[:, :, :], logits[:, :, :], bc(b_bc[:, :].unsqueeze(1), [P, NT, NR]), ALU.add))
            G = lg[:, :, 0:GR]
            E = lg[:, :, GR:NR].rearrange("p t (g e) -> p t g e", g=GR)

            def first_max(out1h, src, m, key, kmax, rev, width):
                ch(V.tensor_reduce(m, src, AX.X, ALU.max))
                ch(V.tensor_tensor(key, src, bc(m.unsqueeze(2), [P, NT, width]), ALU.is_equal))
                ch(V.tensor_tensor(key, key, bc(rev.unsqueeze(1), [P, NT, width]), ALU.mult))
                ch(V.tensor_reduce(kmax, key, AX.X, ALU.max))
                ch(V.tensor_tensor(out1h, key, bc(kmax.unsqueeze(2), [P, NT, width]), ALU.is_equal))

            first_max(ohg[:, :, :], G, gm[:, :], key4[:, :, :], gk[:, :], cst[:, C_REV4:C_REV4 + GR], GR)
            V.tensor_tensor(gs[:, :, :], G, bc(gm[:, :].unsqueeze(2), [P, NT, GR]), ALU.subtract).then_inc(exp_in, 1)
            ch(V.tensor_tensor(sel[:, :, :, :], E, bc(ohg[:, :, :].unsqueeze(3), [P, NT, GR, EG]), ALU.mult))
            ch(V.tensor_reduce(es[:, :, :], sel[:, :, :, :].rearrange("p t g e -> p t e g"), AX.X, ALU.add))
            rev8 = cst[:, C_REV8:C_REV8 + EG]
            first_max(oh[0][:, :, :], es[:, :, :], mx[0][:, :], key8[:, :, :], gk[:, :], rev8, EG)
            ch(V.scalar_tensor_tensor(es2[:, :, :], oh[0][:, :, :], -3.0e38, es[:, :, :], ALU.mult, ALU.add))
            first_max(oh[1][:, :, :], es2[:, :, :], mx[1][:, :], key8[:, :, :], gk[:, :], rev8, EG)
            V.tensor_tensor(ed[:, :], mx[1][:, :], mx[0][:, :], ALU.subtract).then_inc(exp_in, 1)
            for k in range(2):
                ch(V.tensor_tensor(OH[k][:, :, :, :], bc(ohg[:, :, :].unsqueeze(3), [P, NT, GR, EG]),
                                   bc(oh[k][:, :, :].unsqueeze(2), [P, NT, GR, EG]), ALU.mult))
            flat = [OH[k][:, :, :, :].rearrange("p t g e -> p t (g e)") for k in range(2)]
            ch(V.tensor_tensor(O[:, :, :], flat[0], flat[1], ALU.add))
            ch(V.memset(acc[:, 0, :], 0.0))
            for t in range(NT):
                ins = V.tensor_tensor(acc[:, t + 1, :], acc[:, t, :], O[:, t, :], ALU.add)
                if t < NT - 1:
                    ch(ins)
            ins.then_inc(O_ready, 1)
            dve.wait_ge(exp_out, 2)
            ch(V.tensor_reduce(gsum[:, :], gs[:, :, :], AX.X, ALU.add))
            ch(V.reciprocal(gtop[:, :], gsum[:, :]))
            ch(V.tensor_scalar(sd[:, :], ed[:, :], 1.0, None, ALU.add))
            ch(V.reciprocal(sd[:, :], sd[:, :]))
            ch(V.tensor_tensor(w[:, 0, :], gtop[:, :], sd[:, :], ALU.mult))
            ch(V.tensor_tensor(w[:, 1, :], w[:, 0, :], ed[:, :], ALU.mult))
            dve.wait_ge(ranks, 1)
            ch(V.tensor_tensor(cmp_[:, :, :], bc(ps_c[:, 0:NE].unsqueeze(2), [P, NE, NT]),
                               bc(cst[:, C_THR:C_THR + NT].unsqueeze(1), [P, NE, NT]), ALU.is_gt))
            ch(V.tensor_reduce(nblk[:, :], cmp_[:, :, :], AX.X, ALU.add))
            ch(V.tensor_tensor_scan(ends[:, :], cst[:, C_ONES:C_ONES + NE], nblk[:, :], 0.0, ALU.mult, ALU.add))
            ch(V.tensor_tensor(off[:, :], ends[:, :], nblk[:, :], ALU.subtract))
            ch(V.tensor_scalar(off[:, :], off[:, :], float(P), None, ALU.mult))
            ch(V.tensor_tensor(dest[:, :, :], ps_r[:, :, :], bc(off[:, :].unsqueeze(1), [P, NT, NE]), ALU.add))
            for k in range(2):
                ch(V.tensor_tensor(dsel[:, :, :], dest[:, :, :], flat[k], ALU.mult))
                ch(V.tensor_reduce(d[:, k, :], dsel[:, :, :], AX.X, ALU.add))
            ch(V.tensor_copy(di[:, :], d[:, :, :].rearrange("p k t -> p (k t)")))
            ch(V.tensor_single_scalar(hi_i[:, :], di[:, :], 7, ALU.logical_shift_right))
            ch(V.tensor_single_scalar(lo_i[:, :], di[:, :], P - 1, ALU.bitwise_and))
            ch(V.tensor_copy(hi[:, :], hi_i[:, :]))
            ch(V.tensor_copy(lo[:, :], lo_i[:, :]))
            for a in range(32):
                k, t = divmod(a, NT)
                if a >= 2:
                    dve.wait_ge(hot_used, a - 1)
                v = a % 2
                V.tensor_scalar(row1h[:, v, :], iota, lo[:, a:a + 1], None, ALU.is_equal)
                V.tensor_scalar(blk1h[:, v, 0, :], iota[:, 0:64], hi[:, a:a + 1], None, ALU.is_equal)
                V.tensor_scalar(blk1h[:, v, 1, :], iota[:, 0:64], hi[:, a:a + 1],
                                cst[:, C_TOK + t:C_TOK + t + 1], ALU.is_equal, ALU.mult)
                V.tensor_scalar(blk1h[:, v, 2, :], iota[:, 0:64], hi[:, a:a + 1], w[:, k, t:t + 1],
                                ALU.is_equal, ALU.mult).then_inc(hot_ready, 1)
            ch(V.tensor_tensor(bcmp[:, :, :], bc(iota[0:1, 0:64].unsqueeze(2), [1, 64, NE]),
                               bc(ends[0:1, :].unsqueeze(1), [1, 64, NE]), ALU.is_ge))
            ch(V.tensor_reduce(bsum[:, :], bcmp[:, :, :], AX.X, ALU.add))
            ch(V.memset(blk_exp[:, :], 0))
            ch(V.tensor_scalar(blk_exp[:, 0:64], bsum[:, :], float(NE - 1), None, ALU.min))
            ch(V.tensor_scalar(npf[:, :], ends[0:1, NE - 1:NE], -1.0, None, ALU.add))
            ch(V.tensor_copy(npi[:, :], npf[:, :]))
            ch(V.tensor_single_scalar(last_pair[:, :], npi[:, :], 1, ALU.logical_shift_right))
            dve.wait_ge(hot_used, 32)
            ch(V.tensor_copy(tab[:, :, :].rearrange("p c b -> p (c b)"), ps_b[:, 0:192]))
            trash = cst[:, C_TRASH:C_TRASH + 1]
            ch(V.tensor_scalar(tmp[:, :], tab[:, 0, :], trash, None, ALU.mult))
            ch(V.tensor_tensor(tmp[:, :], tab[:, 1, :], tmp[:, :], ALU.subtract))
            ch(V.tensor_scalar(idx_all[:, 0:64], tmp[:, :], trash, None, ALU.add))
            ch(V.tensor_scalar(idx_all[:, 64:BT], iota[:, 0:BT - 64], 0.0, trash, ALU.mult, ALU.add))
            ch(V.tensor_copy(w_all[:, :], tab[:, 2, :]))


NPC = KD + KF


def experts(nc, h2_d, w_pieces, ident_d, idx_all, w_all, blk_exp, last_pair, out):
    with ExitStack() as c:
        sb = lambda n, s, d=F32: c.enter_context(nc.sbuf_tensor(n, s, d))
        sem = lambda n: c.enter_context(nc.semaphore(n))
        wr = sb("ex_w", [P, NPC, D])
        wh, wl = sb("ex_w_hi", [P, NPC, D], F32R), sb("ex_w_lo", [P, NPC, D], F32R)
        xg = sb("ex_xg", [P, 2, D])
        x_hi, x_lo = sb("ex_x_hi", [P, 2, KD, P], F32R), sb("ex_x_lo", [P, 2, KD, P], F32R)
        s, g = sb("ex_s", [P, F]), sb("ex_g", [P, F])
        g_hi, g_lo = sb("ex_g_hi", [P, KF, P], F32R), sb("ex_g_lo", [P, KF, P], F32R)
        y = sb("ex_y", [P, 2, D])
        ix = [sb("ex_ix0", [P, 1], I32), sb("ex_ix1", [P, 1], I32)]
        ident = sb("ex_ident", [P, P])
        ps_h = c.enter_context(nc.psum_tensor("ex_ps_h", [P, 2, F], F32))
        ps_x = c.enter_context(nc.psum_tensor("ex_ps_x", [P, KD, P], F32))
        ps_g = c.enter_context(nc.psum_tensor("ex_ps_g", [P, KF, P], F32))
        ps_y = c.enter_context(nc.psum_tensor("ex_ps_y", [P, D], F32))
        const_in = sem("ex_const_in")
        w_in = [sem(f"ex_w_in{j}") for j in range(NPC)]
        w_rounded, w_split = sem("ex_w_rounded"), sem("ex_w_split")
        w_used = sem("ex_w_used")
        x_in = [sem("ex_x_in0"), sem("ex_x_in1")]
        x_turned, x_rounded, x_split = sem("ex_x_turned"), sem("ex_x_rounded"), sem("ex_x_split")
        ix_ready = sem("ex_ix_ready")
        pool_order = sem("ex_pool_order")
        s_ready, dve_step, g_ready = sem("ex_s_ready"), sem("ex_dve_step"), sem("ex_g_ready")
        g_turned, g_rounded, g_split = sem("ex_g_turned"), sem("ex_g_rounded"), sem("ex_g_split")
        y_read = sem("ex_y_read")
        y_free = sem("ex_y_free")
        added = sem("ex_added")
        block = c.enter_context(nc.Block())

        def rounds(eng, body):
            n = eng.value_load(last_pair[0:1, 0:1], min_val=S // P - 1, max_val=(MAXB - 1) // 2)
            with eng.Fori(0, n) as i:
                body(i, 0, True)
                body(i, 1, True)
            body(n, 0, True)
            body(n, 1, False)

        @block.sync
        def _(sp):
            sp.dma_start(ident[:, :], ident_d).then_inc(const_in, 16)

            def load(b, first):
                e = sp.value_load(blk_exp[0:1, bass.ds(b, 1)], min_val=0, max_val=NE - 1)
                for j in range(NPC):
                    if not first:
                        sp.wait_ge(w_split, b * NPC + (j + 1 - NPC))
                    sp.dma_start(wr[:, j, :], w_pieces[bass.ds(e * NPC + j, 1), :, :]
                                 .rearrange("a p c -> p (a c)")).then_inc(w_in[j], 16)

            load(0, True)
            rounds(sp, lambda i, u, more: load(i * 2 + u + 1, False) if more else None)

        @block.gpsimd
        def _(pool):
            nc.gpsimd.sem_inc(y_free, 2)

            def gather(b, u, first=False):
                nc.gpsimd.tensor_copy(ix[u][:, :], idx_all[:, bass.ds(b, 1)]).then_inc(ix_ready, 1)
                pool.wait_ge(ix_ready, b + 1)
                if not first:
                    pool.wait_ge(x_turned, b)
                nc.gpsimd.sem_inc(pool_order, 1)
                nc.gpsimd.indirect_dma_start(xg[:, u, :], None, h2_d,
                                             bass.IndirectOffsetOnAxis(ap=ix[u][:, 0:1], axis=0)) \
                    .then_inc(x_in[u], 16)

            def add(b, u):
                pool.wait_ge(y_read, b + 2)
                nc.gpsimd.sem_inc(pool_order, 1)
                nc.gpsimd.indirect_dma_start(out, bass.IndirectOffsetOnAxis(ap=ix[u][:, 0:1], axis=0),
                                             y[:, u, :], None, compute_op=ALU.add).then_inc(added, 16)
                pool.wait_ge(added, b * 16 + 16)
                nc.gpsimd.sem_inc(y_free, 1)

            def body(i, u, more):
                if more:
                    gather(i * 2 + u + 1, 1 - u)
                add(i * 2 + u, u)

            gather(0, 0, True)
            rounds(pool, body)

        @block.scalar
        def _(act):
            def round_piece(b, j):
                act.wait_ge(w_in[j], b * 16 + 16)
                if not (isinstance(b, int) and b == 0):
                    act.wait_ge(w_used, b * NPC + (j + 1 - NPC))
                nc.scalar.copy(wh[:, j, :], wr[:, j, :]).then_inc(w_rounded, 1)

            def round_x(b, u):
                act.wait_ge(x_turned, b + 1)
                nc.scalar.copy(x_hi[:, u, :, :], ps_x[:, :, :]).then_inc(x_rounded, 1)

            def sigmoid(b):
                act.wait_ge(w_used, b * NPC + KD)
                nc.scalar.activation(s[:, :], ps_h[:, 0, :], ACT.Sigmoid).then_inc(s_ready, 1)

            def round_g(b):
                act.wait_ge(g_turned, b + 1)
                nc.scalar.copy(g_hi[:, :, :], ps_g[:, :, :]).then_inc(g_rounded, 1)

            def weigh(b, u):
                act.wait_ge(w_used, b * NPC + NPC)
                act.wait_ge(y_free, b + 1)
                nc.scalar.activation(y[:, u, :], ps_y[:, :], ACT.Copy,
                                     scale=w_all[:, bass.ds(b, 1)]).then_inc(y_read, 1)

            def body(i, u, more):
                b = i * 2 + u
                if more:
                    for j in range(4):
                        round_piece(b + 1, j)
                sigmoid(b)
                if more:
                    round_x(b + 1, 1 - u)
                round_g(b)
                if more:
                    for j in range(4, 8):
                        round_piece(b + 1, j)
                weigh(b, u)
                if more:
                    for j in range(8, NPC):
                        round_piece(b + 1, j)

            nc.scalar.sem_inc(y_read, 1)
            round_x(0, 0)
            for j in range(NPC):
                round_piece(0, j)
            rounds(act, body)

        @block.vector
        def _(dve):
            def split_piece(b, j):
                dve.wait_ge(w_rounded, b * NPC + (j + 1))
                nc.vector.tensor_tensor(wl[:, j, :], wr[:, j, :], wh[:, j, :],
                                        ALU.subtract).then_inc(w_split, 1)

            def split_x(b, u):
                dve.wait_ge(x_rounded, b + 1)
                nc.vector.tensor_tensor(x_lo[:, u, :, :], ps_x[:, :, :], x_hi[:, u, :, :],
                                        ALU.subtract).then_inc(x_split, 1)

            def silu(b):
                dve.wait_ge(s_ready, b + 1)
                nc.vector.tensor_tensor(g[:, :], ps_h[:, 0, :], s[:, :], ALU.mult).then_inc(dve_step, 1)
                dve.wait_ge(dve_step, b + 1)
                nc.vector.tensor_tensor(g[:, :], ps_h[:, 1, :], g[:, :], ALU.mult).then_inc(g_ready, 1)

            def split_g(b):
                dve.wait_ge(g_rounded, b + 1)
                nc.vector.tensor_tensor(g_lo[:, :, :], ps_g[:, :, :], g_hi[:, :, :],
                                        ALU.subtract).then_inc(g_split, 1)

            def body(i, u, more):
                b = i * 2 + u
                if more:
                    for j in range(3):
                        split_piece(b + 1, j)
                silu(b)
                if more:
                    split_x(b + 1, 1 - u)
                split_g(b)
                if more:
                    for j in range(3, NPC):
                        split_piece(b + 1, j)

            nc.vector.sem_inc(g_ready, 1)
            split_x(0, 0)
            for j in range(NPC):
                split_piece(0, j)
            rounds(dve, body)

        @block.tensor
        def _(pe):
            pe.wait_ge(const_in, 16)

            def turn_x(b, u):
                pe.wait_ge(x_in[u], b * 8 - u * 8 + 16)
                for k in range(KD):
                    last = nc.tensor.transpose(ps_x[:, k, :], xg[:, u, k * P:(k + 1) * P], ident[:, :])
                last.then_inc(x_turned, 1)

            def up(b, u):
                pe.wait_ge(x_split, b + 1)
                pe.wait_ge(g_ready, b + 1)
                for k in range(KD):
                    pe.wait_ge(w_split, b * NPC + (k + 1))
                    lo = wl[:, k, :]
                    for lhs, rhs, st, sp_ in ((x_hi, wh[:, k, :], k == 0, False), (x_hi, lo, False, False),
                                              (x_lo, wh[:, k, :], False, k == KD - 1)):
                        for m in range(2):
                            last = nc.tensor.matmul(ps_h[:, m, :], lhs[:, u, k, :], rhs[:, m * F:(m + 1) * F],
                                                    start=st, stop=sp_)
                    last.then_inc(w_used, 1)

            def turn_g(b):
                pe.wait_ge(g_ready, b + 2)
                for k in range(KF):
                    last = nc.tensor.transpose(ps_g[:, k, :], g[:, k * P:(k + 1) * P], ident[:, :])
                last.then_inc(g_turned, 1)

            def down(b):
                pe.wait_ge(g_split, b + 1)
                pe.wait_ge(y_read, b + 1)
                for k in range(KF):
                    j = KD + k
                    pe.wait_ge(w_split, b * NPC + (j + 1))
                    lo = wl[:, j, :]
                    for lhs, rhs, st, sp_ in ((g_hi, wh[:, j, :], k == 0, False), (g_hi, lo, False, False),
                                              (g_lo, wh[:, j, :], False, k == KF - 1)):
                        for m in range(2):
                            cols = slice(m * TC, (m + 1) * TC)
                            last = nc.tensor.matmul(ps_y[:, cols], lhs[:, k, :], rhs[:, cols], start=st, stop=sp_)
                    last.then_inc(w_used, 1)

            def body(i, u, more):
                b = i * 2 + u
                up(b, u)
                if more:
                    turn_x(b + 1, 1 - u)
                turn_g(b)
                down(b)

            turn_x(0, 0)
            rounds(pe, body)


def build(nc, x, g1, w_in, b_gate, g_q, g_k, sinks, table, wp, wo, g2, wr, b_all, w_exp,
          ident, pair_ones, neg_ident, mask, onehot, cst, out):
    with ExitStack() as c:
        dram = lambda n, s: nc.dram_tensor(n, s, F32, kind="Internal").ap()
        projF = dram("projF", [NF, P, SPAD])
        qk_hi, qk_lo = dram("qk_hi", [NQK, P, S]), dram("qk_lo", [NQK, P, S])
        gates = dram("gates", [NG, P, S])
        bias_d = dram("band_bias", [8, CHUNK, P])
        yaT, ybT = dram("yaT", [4, P, S]), dram("ybT", [4, P, S])
        mT_hi, mT_lo = dram("mT_hi", [KD, P, S]), dram("mT_lo", [KD, P, S])
        h2 = dram("h2", [OUT_ROWS, D])
        with nc.sbuf_tensor("hT_hi", [P, KD, S], F32R) as hT_hi, nc.sbuf_tensor("hT_lo", [P, KD, S], F32R) as hT_lo:
            norm_transpose(nc, x, g1, ident, hT_hi, hT_lo)
            input_projection(nc, w_in, b_gate, hT_hi, hT_lo, projF, qk_hi, qk_lo, gates)
        band_bias(nc, table, onehot, bias_d)
        banded_attention(nc, projF, g_q, g_k, sinks, bias_d, ident, pair_ones, yaT)
        stick_breaking(nc, projF, qk_hi, qk_lo, ident, neg_ident, mask, ybT)
        merge_branches(nc, yaT, ybT, gates, wp, mT_hi, mT_lo)
        sb = lambda n, s, d: c.enter_context(nc.sbuf_tensor(n, s, d))
        idx_all, w_all = sb("idx_all", [P, BT], I32), sb("w_all", [P, 64], F32)
        blk_exp, last_pair = sb("blk_exp", [1, BT], I32), sb("last_pair", [1, 1], I32)
        with nc.sbuf_tensor("logits", [P, NT, GR + NE], F32) as logits:
            output_projection(nc, mT_hi, mT_lo, wo, x, g2, wr, ident, h2, out, logits)
            routing(nc, logits, b_all, cst, idx_all, w_all, blk_exp, last_pair)
        experts(nc, h2, w_exp, ident, idx_all, w_all, blk_exp, last_pair, out)


def constants():
    f = np.float32
    p = np.arange(P)
    cst = np.zeros((P, CW), f)
    cst[:, C_IOTA:C_IOTA + P] = p
    cst[:, C_REV4:C_REV4 + GR] = np.arange(GR, 0, -1)
    cst[:, C_REV8:C_REV8 + EG] = np.arange(EG, 0, -1)
    cst[:, C_THR:C_THR + NT] = P * np.arange(NT)
    cst[:, C_TOK:C_TOK + NT] = p[:, None] + P * np.arange(NT)
    cst[:, C_TRI:C_TRI + P] = p[:, None] < p[None, :]
    cst[:, C_ONES:C_ONES + P] = 1
    cst[:, C_TRASH] = TRASH + p
    rel = np.arange(CHUNK)[:, None] - np.arange(P)[None, :]
    n = np.abs(rel)
    large = 8 + (np.log(np.maximum(n, 1).astype(f) / f(8)) / f(np.log(16.0)) * f(8)).astype(np.int32)
    bucket = np.where(rel > 0, 16, 0) + np.where(n < 8, n, np.minimum(large, 15))
    onehot = (np.arange(32)[:, None, None] == bucket[None]).astype(f).reshape(32, CHUNK * P)
    return {
        "ident": np.eye(P, dtype=f),
        "pair_ones": np.kron(np.eye(2), np.ones((HD, HD))).astype(f),
        "neg_ident": (-(2.0 ** 100) * np.eye(P)).astype(f),
        "mask": np.tril(np.ones((P, P))).astype(f),
        "onehot": onehot,
        "cst": cst,
    }


def kernel(**inputs):
    import concourse.bacc as bacc
    from concourse.bass_utils import run_bass_kernel_spmd

    a = {k: np.asarray(v) for k, v in inputs.items()}
    w_in = a["w_in"][0]
    aq, akv = 512, 128
    wq = w_in[:, :aq].reshape(D, 2, 4, HD).transpose(0, 2, 1, 3).reshape(D, aq)
    b0 = aq + 2 * akv
    w_cols = np.concatenate([wq, w_in[:, aq:b0], w_in[:, b0 + 1024:b0 + 1536], w_in[:, b0:b0 + 1024],
                             w_in[:, b0 + 1536:]], axis=1)
    wa = a["w_proj_a"][0].reshape(2, 4, HD, D).transpose(1, 0, 2, 3).reshape(512, D)
    wp = np.concatenate([wa, a["w_proj_b"][0]], axis=0)
    rows = lambda w: w.reshape(KD, P, -1).transpose(1, 0, 2)
    tiles = lambda w: w.reshape(KD, P, -1, P).transpose(2, 1, 0, 3)
    w13 = np.concatenate([a["w1"][0].reshape(NE, KD, P, F), a["w3"][0].reshape(NE, KD, P, F)], axis=3)
    w_exp = np.concatenate([w13, a["w2"][0].reshape(NE, KF, P, D)], axis=1).reshape(NE * (KD + KF), P, D)
    arrays = {
        "x": a["x"][0, ::-1],
        "g1": a["norm_mix_g"][0],
        "w_in": tiles(w_cols),
        "b_gate": a["b_gate"][0].reshape(NG, P).T,
        "g_q": a["qa_norm_g"][0].reshape(HD, 1),
        "g_k": a["ka_norm_g"][0].reshape(HD, 1),
        "sinks": a["sinks"][0].reshape(4, 2).T,
        "table": a["rel_bias_table"],
        "wp": tiles(wp),
        "wo": rows(a["w_out"][0]),
        "g2": a["norm_ffn_g"][0],
        "wr": rows(np.concatenate([a["w_group"][0], a["w_router"][0]], axis=1)),
        "b_all": np.concatenate([a["b_group"][0], a["b_router"][0].reshape(-1)]),
        "w_exp": w_exp,
    }
    arrays.update(constants())
    arrays = {k: np.ascontiguousarray(v) for k, v in arrays.items()}
    nc = bacc.Bacc("TRN2", target_bir_lowering=False, num_devices=1)
    aps = {k: nc.dram_tensor("in_" + k, v.shape, mybir.dt.from_np(v.dtype), kind="ExternalInput").ap()
           for k, v in arrays.items()}
    aps["out"] = nc.dram_tensor("out_x", (OUT_ROWS, D), F32, kind="ExternalOutput").ap()
    build(nc, **aps)
    r = run_bass_kernel_spmd(nc, [{"in_" + k: v for k, v in arrays.items()}], core_ids=[0])
    return np.ascontiguousarray(r.results[0]["out_x"][:S][::-1]).reshape(1, S, D)
```

```python
from contextlib import ExitStack

import numpy as np
import concourse.bass as bass
from concourse import mybir

F32 = mybir.dt.float32
F32R = mybir.dt.float32r
BF16 = mybir.dt.bfloat16
I32 = mybir.dt.int32
ACT = mybir.ActivationFunctionType
ALU = mybir.AluOpType
AX = mybir.AxisListType

P = 128
D = 1024
S = 2048
KD = D // P
NT = S // P
TC = 512
NC_ = S // TC
CHUNK = 64
HD = 64
EPS = 1e-6
NF = 10
NQK = 8
NG = 16
SPAD = S + CHUNK
HB = 8
NE = 32
GR = 4
EG = NE // GR
F = 512
KF = F // P
MAXB = 2 * S // P + NE
TRASH = S
OUT_ROWS = S + P


def passes3(nc, out, w_hi, w_lo, x_hi, x_lo, first, last):
    nc.tensor.matmul(out, w_hi, x_hi, start=first, stop=False)
    nc.tensor.matmul(out, w_hi, x_lo, start=False, stop=False)
    return nc.tensor.matmul(out, w_lo, x_hi, start=False, stop=last)


class Chain:

    def __init__(self, eng, sem, base=0):
        self.eng, self.sem, self.base, self.n = eng, sem, base, 0

    def __call__(self, ins):
        self.n += 1
        ins.then_inc(self.sem, 1)
        self.eng.wait_ge(self.sem, self.base + self.n)


def norm_transpose(nc, x, g, ident_d, hT_hi, hT_lo):
    with ExitStack() as c:
        sb = lambda n, s, d=F32: c.enter_context(nc.sbuf_tensor(n, s, d))
        sem = lambda n: c.enter_context(nc.semaphore(n))
        xt = sb("nt_x", [P, 2, D])
        h = sb("nt_h", [P, 2, D])
        junk = sb("nt_sq", [P, D])
        g_bc = sb("nt_g", [P, D])
        ident = sb("nt_ident", [P, P])
        ssq = sb("nt_ssq", [P, 2])
        rms = sb("nt_rms", [P, 2])
        eps = sb("nt_eps", [P, 1])
        rstd = sb("nt_rstd", [P, 2])
        pt = c.enter_context(nc.psum_tensor("nt_ps", [P, 2, KD, P], F32))
        const_in = sem("nt_const_in")
        x_in = [sem("nt_x_in0"), sem("nt_x_in1")]
        x_free = sem("nt_x_free")
        sq_done = sem("nt_sq_done")
        eps_set = sem("nt_eps_set")
        rms_ready = sem("nt_rms_ready")
        rstd_ready = sem("nt_rstd_ready")
        h_ready = sem("nt_h_ready")
        transposed = sem("nt_transposed")
        hi_done = sem("nt_hi_done")
        ps_free = sem("nt_ps_free")
        G = 4
        block = c.enter_context(nc.Block())

        @block.sync
        def _(sp):
            sp.dma_start(g_bc[:, :], g.partition_broadcast(P)).then_inc(const_in, 16)
            sp.dma_start(ident[:, :], ident_d).then_inc(const_in, 16)
            with sp.Fori(0, NT // G) as i:
                for u in range(G):
                    sp.wait_ge(x_free, i * G + u + 1)
                    sp.dma_start(xt[:, u % 2, :], x[bass.ds(i * (G * P) + u * P, P), :]) \
                        .then_inc(x_in[u % 2], 16)

        @block.gpsimd
        def _(pool):
            nc.gpsimd.memset(eps[:, :], EPS).then_inc(eps_set, 1)

        @block.scalar
        def _(act):
            act.wait_ge(eps_set, 1)

            def square(i, u):
                act.wait_ge(x_in[u % 2], (i * (G // 2) + u // 2 + 1) * 16)
                nc.scalar.activation(junk[:, :], xt[:, u % 2, :], ACT.Square,
                                     accum_out=ssq[:, u % 2:u % 2 + 1]).then_inc(sq_done, 1)
                act.wait_ge(sq_done, i * G + u + 1)
                nc.scalar.activation(rms[:, u % 2:u % 2 + 1], ssq[:, u % 2:u % 2 + 1], ACT.Sqrt,
                                     scale=1.0 / D, bias=eps[:, :]).then_inc(rms_ready, 1)

            def take_hi(i, u):
                act.wait_ge(transposed, i * G + u + 3)
                nc.scalar.copy(hT_hi[:, :, bass.ds(i * (G * P) + u * P, P)], pt[:, u % 2, :, :]) \
                    .then_inc(hi_done, 1)

            with act.Fori(0, NT // G) as i:
                square(i, 0)
                square(i, 1)
                for u in range(G):
                    take_hi(i, u)
                    if u + 2 < G:
                        square(i, u + 2)

        @block.vector
        def _(dve):
            nc.vector.sem_inc(x_free, 2)
            nc.vector.sem_inc(ps_free, 2)
            dve.wait_ge(const_in, 32)

            def normalise(i, u):
                v = u % 2
                dve.wait_ge(rms_ready, i * G + u + 1)
                nc.vector.reciprocal(rstd[:, v:v + 1], rms[:, v:v + 1]).then_inc(rstd_ready, 1)
                dve.wait_ge(rstd_ready, i * G + u + 1)
                dve.wait_ge(transposed, i * G + u + 1)
                nc.vector.scalar_tensor_tensor(h[:, v, :], xt[:, v, :], rstd[:, v:v + 1], g_bc[:, :],
                                               ALU.mult, ALU.mult).then_inc(h_ready, 1)
                dve.wait_ge(h_ready, i * G + u + 1)
                nc.vector.sem_inc(x_free, 1)

            def take_lo(i, u):
                dve.wait_ge(hi_done, i * G + u + 1)
                sl = bass.ds(i * (G * P) + u * P, P)
                nc.vector.tensor_tensor(hT_lo[:, :, sl], pt[:, u % 2, :, :], hT_hi[:, :, sl],
                                        ALU.subtract).then_inc(ps_free, 1)

            with dve.Fori(0, NT // G) as i:
                normalise(i, 0)
                normalise(i, 1)
                for u in range(G):
                    take_lo(i, u)
                    if u + 2 < G:
                        normalise(i, u + 2)

        @block.tensor
        def _(pe):
            nc.tensor.sem_inc(transposed, 2)
            pe.wait_ge(const_in, 32)
            with pe.Fori(0, NT // G) as i:
                for u in range(G):
                    pe.wait_ge(h_ready, i * G + u + 1)
                    pe.wait_ge(ps_free, i * G + u + 1)
                    for k in range(KD):
                        last = nc.tensor.transpose(pt[:, u % 2, k, :], h[:, u % 2, k * P:(k + 1) * P],
                                                   ident[:, :])
                    last.then_inc(transposed, 1)


def input_projection(nc, w_tiles, b_gate, hT_hi, hT_lo, projF, qk_hi, qk_lo, gates):
    with ExitStack() as c:
        sb = lambda n, s, d=F32: c.enter_context(nc.sbuf_tensor(n, s, d))
        sem = lambda n: c.enter_context(nc.semaphore(n))
        w = sb("ip_w", [P, 2, KD, P])
        w_hi = sb("ip_w_hi", [P, 2, KD, P], F32R)
        w_lo = sb("ip_w_lo", [P, 2, KD, P], F32R)
        o = sb("ip_out", [P, 2, S])
        o_hi = o[:, :, :].bitcast(F32R)
        o_lo = sb("ip_out_lo", [P, 2, S], F32R)
        bias = sb("ip_bias", [P, NG])
        zero = sb("ip_zero", [P, CHUNK])
        ps = c.enter_context(nc.psum_tensor("ip_ps", [P, 2, S], F32))
        w_in = [sem("ip_w_in0"), sem("ip_w_in1")]
        w_split = sem("ip_w_split")
        hi_done = sem("ip_w_hi_done")
        mm_done = sem("ip_mm_done")
        read_out = sem("ip_read_out")
        out_hi = sem("ip_out_hi")
        stored = [sem("ip_stored0"), sem("ip_stored1")]
        bias_in = sem("ip_bias_in")
        zero_set = sem("ip_zero_set")
        pads = sem("ip_pads")
        block = c.enter_context(nc.Block())
        NTL = NF + NQK + NG
        LAST = NTL // 2 - 1
        PARTS = [(0, NF // 2, "f32"), (NF // 2, (NF + NQK) // 2, "split"),
                 ((NF + NQK) // 2, LAST, "gate")]

        @block.sync
        def _(sp):
            sp.dma_start(bias[:, :], b_gate).then_inc(bias_in, 16)
            with sp.Fori(0, NTL // 2) as i:
                for u in range(2):
                    sp.wait_ge(w_split, i * 2 + u + 1)
                    sp.dma_start(w[:, u, :, :], w_tiles[bass.ds(i * 2 + u, 1), :, :, :]
                                 .rearrange("a p k c -> p (a k) c")).then_inc(w_in[u], 16)

        @block.gpsimd
        def _(pool):
            nc.gpsimd.memset(zero[:, :], 0.0).then_inc(zero_set, 1)
            pool.wait_ge(zero_set, 1)
            for t in (4, 5):
                pool.dma_start(projF[t, :, S:SPAD], zero[:, :]).then_inc(pads, 16)
            pool.wait_ge(pads, 32)

        @block.vector
        def _(dve):
            nc.vector.sem_inc(w_split, 2)

            def split_weight(n, u):
                dve.wait_ge(w_in[u], n * 8 - u * 8 + 16)
                dve.wait_ge(hi_done, n + 1)
                nc.vector.tensor_tensor(w_lo[:, u, :, :], w[:, u, :, :], w_hi[:, u, :, :],
                                        ALU.subtract).then_inc(w_split, 1)

            def read_lo(n, u):
                dve.wait_ge(out_hi, n - NF + 1)
                nc.vector.tensor_tensor(o_lo[:, u, :], ps[:, u, :], o_hi[:, u, :],
                                        ALU.subtract).then_inc(read_out, 1)

            split_weight(0, 0)
            split_weight(1, 1)
            for first, end, kind in PARTS:
                with dve.Fori(first, end) as i:
                    for u in range(2):
                        split_weight(i * 2 + u + 2, u)
                        if kind == "split":
                            read_lo(i * 2 + u, u)

        @block.scalar
        def _(act):
            nc.scalar.sem_inc(read_out, 2)
            act.wait_ge(bias_in, 16)

            def round_weight(n, u):
                act.wait_ge(w_in[u], n * 8 - u * 8 + 16)
                act.wait_ge(mm_done, n + 1)
                nc.scalar.copy(w_hi[:, u, :, :], w[:, u, :, :]).then_inc(hi_done, 1)

            def read(kind, i, u):
                n = i * 2 + u
                act.wait_ge(mm_done, n + 3)
                if kind == "f32":
                    done = i * 16 + 16
                elif kind == "split":
                    done = i * 32 + (16 - NF // 2 * 16)
                else:
                    done = i * 16 + (16 + NQK // 2 * 16)
                act.wait_ge(stored[u], done)
                src = ps[:, u, :]
                if kind == "f32":
                    nc.scalar.copy(o[:, u, :], src).then_inc(read_out, 1)
                    act.wait_ge(read_out, n + 3)
                    act.dma_start(projF[bass.ds(n, 1), :, 0:S].rearrange("a p s -> p (a s)"), o[:, u, :]) \
                        .then_inc(stored[u], 16)
                elif kind == "gate":
                    nc.scalar.activation(o[:, u, :], src, ACT.Sigmoid,
                                         bias=bias[:, bass.ds(n - (NF + NQK), 1)]).then_inc(read_out, 1)
                    act.wait_ge(read_out, n + 3)
                    act.dma_start(gates[bass.ds(n - (NF + NQK), 1), :, :].rearrange("a p s -> p (a s)"),
                                  o[:, u, :]).then_inc(stored[u], 16)
                else:
                    nc.scalar.copy(o_hi[:, u, :], src).then_inc(out_hi, 1)
                    act.wait_ge(read_out, n + 3)
                    for dst, part in ((qk_hi, o), (qk_lo, o_lo[:, :, :].bitcast(F32))):
                        act.dma_start(dst[bass.ds(n - NF, 1), :, :].rearrange("a p s -> p (a s)"),
                                      part[:, u, :]).then_inc(stored[u], 16)

            nc.scalar.sem_inc(stored[0], 16)
            nc.scalar.sem_inc(stored[1], 16)
            round_weight(0, 0)
            round_weight(1, 1)
            for first, end, kind in PARTS:
                with act.Fori(first, end) as i:
                    for u in range(2):
                        round_weight(i * 2 + u + 2, u)
                        read(kind, i, u)
            for u in range(2):
                read("gate", LAST, u)
            for u in range(2):
                act.wait_ge(stored[u], 16 + (NTL + NQK) // 2 * 16)

        @block.tensor
        def _(pe):
            nc.tensor.sem_inc(mm_done, 2)
            with pe.Fori(0, NTL // 2) as i:
                for u in range(2):
                    pe.wait_ge(w_split, i * 2 + u + 3)
                    pe.wait_ge(read_out, i * 2 + u + 1)
                    for t in range(NC_):
                        cols = slice(t * TC, (t + 1) * TC)
                        for k in range(KD):
                            last = passes3(nc, ps[:, u, cols], w_hi[:, u, k, :], w_lo[:, u, k, :],
                                           hT_hi[:, k, cols], hT_lo[:, k, cols], k == 0, k == KD - 1)
                    last.then_inc(mm_done, 1)


def band_bias(nc, table, onehot, bias_d):
    with ExitStack() as c:
        sb = lambda n, s, d=F32: c.enter_context(nc.sbuf_tensor(n, s, d))
        sem = lambda n: c.enter_context(nc.semaphore(n))
        NB = 32
        tab = sb("bb_tab", [2 * NB, 8])
        hi, pair = sb("bb_hi", [2 * NB, 8], F32R), sb("bb_pair", [2 * NB, 8], F32R)
        oh = sb("bb_onehot", [2 * NB, CHUNK * P], F32R)
        line = sb("bb_line", [8, CHUNK * P])
        ps = c.enter_context(nc.psum_tensor("bb_ps", [P, 2, TC], F32))
        loaded, mm, read, stored = sem("bb_loaded"), sem("bb_mm"), sem("bb_read"), sem("bb_stored")
        oh_in, split = sem("bb_oh_in"), sem("bb_split")
        block = c.enter_context(nc.Block())
        n_mm = CHUNK * P // TC

        @block.sync
        def _(sp):
            for half in range(2):
                sp.dma_start(tab[half * NB:(half + 1) * NB, :], table).then_inc(loaded, 16)
            sp.wait_ge(read, n_mm)
            sp.dma_start(bias_d.rearrange("h i j -> h (i j)"), line[:, :]).then_inc(stored, 16)
            sp.wait_ge(stored, 16)

        @block.gpsimd
        def _(pool):
            for half in range(2):
                pool.dma_start(oh[half * NB:(half + 1) * NB, :], onehot).then_inc(oh_in, 16)

        @block.tensor
        def _(pe):
            pe.wait_ge(oh_in, 32)
            pe.wait_ge(split, 3)
            for m in range(n_mm):
                if m >= 2:
                    pe.wait_ge(read, m - 1)
                nc.tensor.matmul(ps[0:8, m % 2, :], pair[:, :], oh[:, m * TC:(m + 1) * TC],
                                 start=True, stop=True).then_inc(mm, 1)

        @block.vector
        def _(dve):
            dve.wait_ge(loaded, 32)
            nc.vector.tensor_copy(hi[:, :], tab[:, :]).then_inc(split, 1)
            dve.wait_ge(split, 1)
            nc.vector.tensor_copy(pair[0:NB, :], hi[0:NB, :]).then_inc(split, 1)
            nc.vector.tensor_tensor(pair[NB:, :], tab[NB:, :], hi[NB:, :], ALU.subtract).then_inc(split, 1)
            for m in range(n_mm):
                dve.wait_ge(mm, m + 1)
                nc.vector.tensor_copy(line[:, m * TC:(m + 1) * TC], ps[0:8, m % 2, :]).then_inc(read, 1)


def banded_attention(nc, projF, g_q, g_k, sinks, bias_d, ident_d, pair_ones, yaT):
    with ExitStack() as c:
        sb = lambda n, s, d=F32: c.enter_context(nc.sbuf_tensor(n, s, d))
        sem = lambda n: c.enter_context(nc.semaphore(n))
        KW = P + CHUNK
        q = sb("ba_q", [P, 2, 4, P])
        k = sb("ba_k", [P, 2, KW])
        v = sb("ba_v", [P, 2, KW])
        qsq = sb("ba_qsq", [P, 4, P])
        ksq = sb("ba_ksq", [P, KW])
        rq = sb("ba_rq", [P, 4, P])
        rk = sb("ba_rk", [P, KW])
        lnq = sb("ba_lnq", [P, 4, P])
        lnk = sb("ba_lnk", [P, KW])
        qn = sb("ba_qn", [P, 2, 4, CHUNK])
        kn = sb("ba_kn", [P, KW])
        vn = sb("ba_vn", [P, 2, 2, P])
        s = sb("ba_s", [P, 2, 2, 4, P])
        e = sb("ba_e", [P, 8, P])
        pT = sb("ba_pT", [P, 2, 4 * P])
        o = sb("ba_o", [P, 2, 4, 2, CHUNK])
        bias = sb("ba_bias", [P, 4, P])
        bias_end = sb("ba_bias_end", [P, 4, P])
        sink = sb("ba_sink", [P, 2, 4])
        gq, gk = sb("ba_gq", [P, 1]), sb("ba_gk", [P, 1])
        eps = sb("ba_eps", [P, 1])
        ident, ones = sb("ba_ident", [P, P]), sb("ba_ones", [P, P])
        mx, negm, sneg = sb("ba_mx", [P, 8]), sb("ba_negm", [P, 8]), sb("ba_sneg", [P, 8])
        esink, rowsum = sb("ba_esink", [P, 8]), sb("ba_rowsum", [P, 8])
        den, rden = sb("ba_den", [P, 8]), sb("ba_rden", [P, 8])
        pb = lambda n, sh: c.enter_context(nc.psum_tensor(n, sh, F32))
        ps_q, ps_k = pb("ba_ps_q", [P, 4, P]), pb("ba_ps_k", [P, TC])
        ps_v = pb("ba_ps_v", [P, 4, P])
        ps_s = pb("ba_ps_s", [P, 2, 2, 2, P])
        ps_t = pb("ba_ps_t", [P, 2, 4 * P])
        ps_o = pb("ba_ps_o", [P, 2, 4 * CHUNK])
        const_in, prep = sem("ba_const_in"), sem("ba_prep")
        loaded = [sem("ba_loaded0"), sem("ba_loaded1")]
        squared, ssq_done = sem("ba_squared"), sem("ba_ssq_done")
        act_step, dve_step = sem("ba_act_step"), sem("ba_dve_step")
        r_ready, qk_ready = sem("ba_r_ready"), sem("ba_qk_ready")
        v_turned, vn_ready = sem("ba_v_turned"), sem("ba_vn_ready")
        scored, s_ready = sem("ba_scored"), sem("ba_s_ready")
        max_ready, exp_done, p_ready = sem("ba_max_ready"), sem("ba_exp_done"), sem("ba_p_ready")
        p_turned, pT_ready = sem("ba_p_turned"), sem("ba_pT_ready")
        pv_done, o_ready = sem("ba_pv_done"), sem("ba_o_ready")
        stored = [sem("ba_stored0"), sem("ba_stored1")]
        block = c.enter_context(nc.Block())
        N = NT
        PAIRS = N // 2 - 1

        @block.sync
        def _(sp):
            for h2 in range(2):
                half = slice(h2 * CHUNK, (h2 + 1) * CHUNK)
                sp.dma_start(bias[half, :, :], bias_d.rearrange("(a b) i j -> b i a j", b=2)[h2]) \
                    .then_inc(const_in, 16)
                sp.dma_start(sink[half, 0, :], sinks[h2, :]
                             .partition_broadcast(CHUNK)).then_inc(const_in, 16)
                sp.dma_start(gq[half, :], g_q).then_inc(const_in, 16)
                sp.dma_start(gk[half, :], g_k).then_inc(const_in, 16)
            sp.dma_start(ident[:, :], ident_d).then_inc(const_in, 16)
            sp.dma_start(ones[:, :], pair_ones).then_inc(const_in, 16)

            with sp.Fori(0, N // 2) as i:
                for u in range(2):
                    sp.wait_ge(o_ready, i * 2 + u + 2)
                    sp.dma_start(yaT[:, :, bass.ds(i * (2 * P) + u * P, P)].rearrange("t p s -> p t s"),
                                   o[:, u, :, :, :].rearrange("p t c s -> p t (c s)")) \
                        .then_inc(stored[u], 16)
            for u in range(2):
                sp.wait_ge(stored[u], 16 + N // 2 * 16)

        @block.gpsimd
        def _(pool):
            def load(n, u):
                pool.dma_start(q[:, u, :, :], projF[0:4, :, bass.ds(n * P, P)].rearrange("t p s -> p t s")) \
                    .then_inc(loaded[u], 16)
                pool.dma_start(k[:, u, :], projF[4, :, bass.ds(n * P, KW)]).then_inc(loaded[u], 16)
                pool.dma_start(v[:, u, :], projF[5, :, bass.ds(n * P, KW)]).then_inc(loaded[u], 16)

            load(0, 0)
            load(1, 1)
            with pool.Fori(1, N // 2) as i:
                for u in range(2):
                    pool.wait_ge(qk_ready, i * 2 + u - 1)
                    pool.wait_ge(v_turned, i * 2 + u - 1)
                    load(i * 2 + u, u)

        @block.scalar
        def _(act):
            act.wait_ge(const_in, 160)
            act.wait_ge(prep, 2)

            def squares(n, u):
                act.wait_ge(loaded[u], n * 24 - u * 24 + 48)
                if not (isinstance(n, int) and n == 0):
                    act.wait_ge(ssq_done, n)
                nc.scalar.activation(qsq[:, :, :], q[:, u, :, :], ACT.Square).then_inc(act_step, 1)
                nc.scalar.activation(ksq[:, :], k[:, u, :], ACT.Square).then_inc(squared, 1)
                act.wait_ge(act_step, n * 4 + 1)

            def rstd(n, u):
                act.wait_ge(ssq_done, n + 1)
                nc.scalar.activation(lnq[:, :, :], ps_q[:, :, :], ACT.Ln, scale=1.0 / HD,
                                     bias=eps[:, :]).then_inc(act_step, 1)
                nc.scalar.activation(lnk[:, :], ps_k[:, 0:KW], ACT.Ln, scale=1.0 / HD,
                                     bias=eps[:, :]).then_inc(act_step, 1)
                act.wait_ge(act_step, n * 4 + 3)
                if not (isinstance(n, int) and n == 0):
                    act.wait_ge(qk_ready, n)
                nc.scalar.activation(rq[:, :, :], lnq[:, :, :], ACT.Exp, scale=-0.5).then_inc(act_step, 1)
                nc.scalar.activation(rk[:, :], lnk[:, :], ACT.Exp, scale=-0.5).then_inc(r_ready, 1)
                act.wait_ge(act_step, n * 4 + 4)

            def take_v(n, u):
                act.wait_ge(v_turned, n + 1)
                if not (isinstance(n, int) and n == 0):
                    act.wait_ge(pv_done, n)
                nc.scalar.copy(vn[:, u, :, :], ps_v[:, 0:2, :]).then_inc(vn_ready, 1)

            def exps(n, u):
                act.wait_ge(max_ready, n + 1)
                for a in range(8):
                    nc.scalar.activation(e[:, a, :], s[:, u, a // 4, a % 4, :], ACT.Exp,
                                         bias=negm[:, a:a + 1], accum_out=rowsum[:, a:a + 1])
                nc.scalar.activation(esink[:, :], sneg[:, :], ACT.Exp).then_inc(exp_done, 1)

            def take_pT(n, u):
                for cc in range(2):
                    act.wait_ge(p_turned, n * 2 + cc + 1)
                    nc.scalar.copy(pT[:, cc, :], ps_t[:, cc, :]).then_inc(pT_ready, 1)

            def step(n, u, norm=True, score=True):
                exps(n, u)
                if norm:
                    squares(n + 2, u)
                if score:
                    take_v(n + 1, 1 - u)
                take_pT(n, u)
                if norm:
                    rstd(n + 2, u)

            nc.scalar.sem_inc(pT_ready, 2)
            squares(0, 0)
            rstd(0, 0)
            take_v(0, 0)
            squares(1, 1)
            rstd(1, 1)
            with act.Fori(0, PAIRS) as i:
                for u in range(2):
                    step(i * 2 + u, u)
            step(N - 2, 0, norm=False)
            step(N - 1, 1, norm=False, score=False)

        @block.vector
        def _(dve):
            nc.vector.memset(eps[:, :], EPS).then_inc(prep, 1)
            dve.wait_ge(const_in, 160)
            chain = Chain(dve, dve_step)
            chain(nc.vector.tensor_copy(bias_end[:, :, :], bias[:, :, :]))
            chain(nc.vector.memset(bias_end[:, :, CHUNK:P], -1.0e30))
            nc.vector.tensor_copy(sink[:, 1, :], sink[:, 0, :]).then_inc(prep, 1)
            dve.wait_ge(prep, 2)
            STEPS = 6

            def norms(n, u):
                dve.wait_ge(r_ready, n + 1)
                if not (isinstance(n, int) and n == 0):
                    dve.wait_ge(scored, n)
                for cc in range(2):
                    own = slice(cc * CHUNK, (cc + 1) * CHUNK)
                    nc.vector.scalar_tensor_tensor(qn[:, cc, :, :], q[:, u, :, own], gq[:, :],
                                                   rq[:, :, own], ALU.mult, ALU.mult)
                nc.vector.scalar_tensor_tensor(kn[:, :], k[:, u, :], gk[:, :], rk[:, :],
                                               ALU.mult, ALU.mult).then_inc(qk_ready, 1)

            def take_scores(n, u, last=False):
                dve.wait_ge(scored, n + 1)
                for g in range(2):
                    for cc in range(2):
                        b = bias_end if last and cc else bias
                        ins = nc.vector.scalar_tensor_tensor(
                            s[:, u, cc, 2 * g:2 * g + 2, :], ps_s[:, g, cc, :, :], HD ** -0.5,
                            b[:, 2 * g:2 * g + 2, :], ALU.mult, ALU.add)
                ins.then_inc(s_ready, 1)

            def maxima(n, u, chain):
                dve.wait_ge(s_ready, n + 1)
                chain(nc.vector.tensor_reduce(mx[:, :], s[:, u, :, :, :].rearrange("p c t s -> p (c t) s"),
                                              AX.X, ALU.max))
                chain(nc.vector.tensor_tensor(mx[:, :], mx[:, :], sink[:, :, :].rearrange("p c t -> p (c t)"),
                                              ALU.max))
                chain(nc.vector.tensor_scalar(negm[:, :], mx[:, :], -1.0, None, ALU.mult))
                nc.vector.tensor_tensor(sneg[:, :], negm[:, :], sink[:, :, :].rearrange("p c t -> p (c t)"),
                                        ALU.add).then_inc(max_ready, 1)

            def probs(n, u, chain):
                dve.wait_ge(exp_done, n + 1)
                chain(nc.vector.tensor_tensor(den[:, :], rowsum[:, :], esink[:, :], ALU.add))
                chain(nc.vector.reciprocal(rden[:, :], den[:, :]))
                nc.vector.tensor_tensor(e[:, :, :], e[:, :, :],
                                        rden[:, :].unsqueeze(2).to_broadcast([P, 8, P]), ALU.mult) \
                    .then_inc(p_ready, 1)

            def take_o(n, u):
                dve.wait_ge(pv_done, n + 2)
                dve.wait_ge(stored[u], n * 8 - u * 8 + 16)
                nc.vector.tensor_copy(o[:, u, :, :, :].rearrange("p t c s -> p c t s"),
                                      ps_o[:, :, :].rearrange("p c (t s) -> p c t s", t=4)) \
                    .then_inc(o_ready, 1)

            def step(n, u, score=True, last=False):
                chain = Chain(dve, dve_step, n * (STEPS - 1) + 2)
                maxima(n, u, chain)
                if score:
                    norms(n + 1, 1 - u)
                probs(n, u, chain)
                if score:
                    take_scores(n + 1, 1 - u, last)
                take_o(n, u)

            norms(0, 0)
            take_scores(0, 0)
            nc.vector.sem_inc(stored[0], 16)
            nc.vector.sem_inc(stored[1], 16)
            nc.vector.sem_inc(o_ready, 1)
            with dve.Fori(0, PAIRS) as i:
                for u in range(2):
                    step(i * 2 + u, u)
            step(N - 2, 0, last=True)
            step(N - 1, 1, score=False)

        @block.tensor
        def _(pe):
            nc.tensor.sem_inc(pv_done, 1)
            pe.wait_ge(const_in, 160)

            def sums(n, u):
                pe.wait_ge(squared, n + 1)
                if not (isinstance(n, int) and n == 0):
                    pe.wait_ge(r_ready, n)
                nc.tensor.matmul(ps_q[:, :, :], ones[:, :], qsq[:, :, :], start=True, stop=True)
                nc.tensor.matmul(ps_k[:, 0:KW], ones[:, :], ksq[:, :], start=True, stop=True) \
                    .then_inc(ssq_done, 1)

            def turn_v(n, u):
                if not (isinstance(n, int) and n == 0):
                    pe.wait_ge(vn_ready, n)
                for cc in range(2):
                    last = nc.tensor.transpose(ps_v[:, cc, :], v[:, u, cc * CHUNK:cc * CHUNK + P], ident[:, :])
                last.then_inc(v_turned, 1)

            def scores(n, u):
                pe.wait_ge(qk_ready, n + 1)
                if not (isinstance(n, int) and n == 0):
                    pe.wait_ge(s_ready, n)
                for cc in range(2):
                    for pr in range(2):
                        for g in range(2):
                            rows = slice(g * HD, (g + 1) * HD)
                            last = nc.tensor.matmul(ps_s[:, g, cc, pr, :],
                                                    qn[rows, cc, 2 * pr:2 * pr + 2, :]
                                                    .rearrange("p t s -> p (t s)"),
                                                    kn[rows, cc * CHUNK:cc * CHUNK + P], start=True, stop=True)
                last.then_inc(scored, 1)

            def turn_p(n, u):
                pe.wait_ge(p_ready, n + 1)
                for cc in range(2):
                    pe.wait_ge(pT_ready, n * 2 + cc + 1)
                    for a in range(4):
                        last = nc.tensor.transpose(ps_t[:, cc, a * P:(a + 1) * P], e[:, cc * 4 + a, :], ident[:, :])
                    last.then_inc(p_turned, 1)

            def products(n, u):
                pe.wait_ge(vn_ready, n + 1)
                pe.wait_ge(o_ready, n + 1)
                for cc in range(2):
                    pe.wait_ge(pT_ready, n * 2 + cc + 3)
                    for g in range(2):
                        last = nc.tensor.matmul(ps_o[g * HD:(g + 1) * HD, cc, :], vn[:, u, cc, g * HD:(g + 1) * HD],
                                                pT[:, cc, g * 2 * P:(g + 1) * 2 * P], start=True, stop=True)
                last.then_inc(pv_done, 1)

            def step(n, u, norm=True, score=True):
                if score:
                    scores(n + 1, 1 - u)
                    turn_v(n + 1, 1 - u)
                if norm:
                    sums(n + 2, u)
                turn_p(n, u)
                products(n, u)

            sums(0, 0)
            turn_v(0, 0)
            scores(0, 0)
            sums(1, 1)
            with pe.Fori(0, PAIRS) as i:
                for u in range(2):
                    step(i * 2 + u, u)
            step(N - 2, 0, norm=False)
            step(N - 1, 1, norm=False, score=False)


def stick_breaking(nc, projF, qk_hi, qk_lo, ident_d, neg_ident, mask_d, ybT):
    UNITS = [(t, off, min(TC, S - P * t - off)) for t in range(NT) for off in range(0, S - P * t, TC)]
    NU = len(UNITS)
    BODY = [(u, t, off, w) for u in range(2) for t, off, w in UNITS]
    NBODY = 2 * NU
    CR = 4
    ends = [j for j, (_, t, off, w) in enumerate(BODY) if t % 4 == 3 and P * t + off + w == S]
    last_unit = {(u, t): j for j, (u, t, _, _) in enumerate(BODY)}
    by_act = [j % 5 == 2 for j in range(NBODY)]
    with ExitStack() as c:
        sb = lambda n, s, d=F32: c.enter_context(nc.sbuf_tensor(n, s, d))
        sem = lambda n: c.enter_context(nc.semaphore(n))
        qs = sb("sb_q", [P, 2, S], F32R)
        kh = sb("sb_kh", [P, 2, S], F32R)
        kl = sb("sb_kl", [P, 2, S], F32R)
        vT = sb("sb_vT", [P, S])
        v = sb("sb_v", [P, NT, P])
        sig = sb("sb_sig", [P, 4, TC])
        R = sb("sb_R", [P, 2, S + 1])
        aT = sb("sb_aT", [P, 2, TC])
        y = sb("sb_y", [HD, 2, TC])
        zeros = sb("sb_zeros", [P, TC])
        ident = sb("sb_ident", [P, P])
        nident, mask = sb("sb_nident", [P, P], BF16), sb("sb_mask", [P, P], BF16)
        stage = sb("sb_stage", [P, 2, P])
        z = c.enter_context(nc.psum_tensor("sb_z", [P, 3, TC], F32))
        ps_t = c.enter_context(nc.psum_tensor("sb_pst", [P, 2, TC], F32))
        ps_v = c.enter_context(nc.psum_tensor("sb_psv", [P, TC], F32))
        ps_y = c.enter_context(nc.psum_tensor("sb_psy", [P, 2, TC], F32))
        const_in, prep = sem("sb_const_in"), sem("sb_prep")
        head_in = [sem("sb_head_in0"), sem("sb_head_in1")]
        v_in = sem("sb_v_in")
        v_turned, v_ready = sem("sb_v_turned"), sem("sb_v_ready")
        z_done, sig_done, scan_done = sem("sb_z_done"), sem("sb_sig_done"), sem("sb_scan_done")
        a_done, t_done = sem("sb_a_done"), sem("sb_t_done")
        aT_act, aT_dve = sem("sb_aT_act"), sem("sb_aT_dve")
        y_done, y_read = sem("sb_y_done"), sem("sb_y_read")
        stored = [sem("sb_stored0"), sem("sb_stored1")]
        block = c.enter_context(nc.Block())
        ROUNDS = HB // 2

        def unit(eng, s, i, j):
            eng.wait_ge(s, i * NBODY + (CR + j + 1))

        @block.sync
        def _(sp):
            sp.dma_start(ident[:, :], ident_d).then_inc(const_in, 16)
            sp.dma_start(stage[:, 0, :], neg_ident).then_inc(const_in, 16)
            sp.dma_start(stage[:, 1, :], mask_d).then_inc(const_in, 16)
            sp.sem_inc(stored[0], 16)
            sp.sem_inc(stored[1], 16)

            def load_v(i):
                sp.dma_start(vT[:, :], projF[bass.ds(i + 6, 1), :, 0:S].rearrange("a p s -> p (a s)")) \
                    .then_inc(v_in, 16)

            def store(i, m):
                sp.wait_ge(y_read, i * 8 + (m + 1 + CR))
                u, g = divmod(m, 4)
                sp.dma_start(ybT[bass.ds(i, 1), u * HD:(u + 1) * HD, g * TC:(g + 1) * TC]
                             .rearrange("a p s -> p (a s)"), y[:, m % 2, :]).then_inc(stored[m % 2], 16)

            load_v(0)
            with sp.Fori(0, ROUNDS - 1) as i:
                for m in range(8):
                    store(i, m)
                    if m == 3:
                        load_v(i + 1)
            for m in range(8):
                store(ROUNDS - 1, m)
            for b in range(2):
                sp.wait_ge(stored[b], 16 + ROUNDS * 4 * 16)

        @block.scalar
        def _(act):
            nc.scalar.sem_inc(sig_done, CR)
            nc.scalar.sem_inc(y_read, CR)

            def sigmoids(i, j):
                _, t, off, w = BODY[j]
                unit(act, z_done, i, j)
                unit(act, t_done, i, j - 4)
                nc.scalar.activation(sig[:, j % 4, 0:w], z[:, j % 3, 0:w], ACT.Sigmoid, scale=HD ** -0.5)
                nc.scalar.activation(z[:, j % 3, 0:w], z[:, j % 3, 0:w], ACT.Sigmoid, scale=-HD ** -0.5) \
                    .then_inc(sig_done, 1)

            def take_v(i, b):
                act.wait_ge(v_turned, i * 4 + (b + 1))
                nc.scalar.copy(v[:, 4 * b:4 * b + 4, :].rearrange("p t d -> p (t d)"), ps_v[:, :]) \
                    .then_inc(v_ready, 1)

            def take_y(i, m):
                act.wait_ge(y_done, i * 8 + (m + 1))
                act.wait_ge(stored[m % 2], i * 64 + (m // 2 * 16 + 16))
                nc.scalar.copy(y[:, m % 2, :], ps_y[0:HD, m % 2, :]).then_inc(y_read, 1)

            with act.Fori(0, ROUNDS) as i:
                for j in range(NBODY + 7):
                    if j < 4:
                        take_v(i, j)
                    if j < NBODY:
                        sigmoids(i, j)
                    if 0 <= j - 3 < NBODY and by_act[j - 3]:
                        w = BODY[j - 3][3]
                        unit(act, t_done, i, j - 3)
                        nc.scalar.copy(aT[:, (j - 3) % 2, 0:w], ps_t[:, (j - 3) % 2, 0:w]).then_inc(aT_act, 1)
                    if j - 6 in ends:
                        take_y(i, ends.index(j - 6))

        @block.vector
        def _(dve):
            nc.vector.sem_inc(scan_done, CR)
            nc.vector.memset(zeros[:, :], 0.0)
            nc.vector.memset(R[:, :, 0:1], 1.0).then_inc(prep, 1)
            dve.wait_ge(const_in, 48)
            nc.vector.tensor_copy(nident[:, :], stage[:, 0, :])
            nc.vector.tensor_copy(mask[:, :], stage[:, 1, :]).then_inc(prep, 1)
            dve.wait_ge(prep, 2)

            def scan(i, j):
                u, t, off, w = BODY[j]
                unit(dve, sig_done, i, j)
                if off:
                    unit(dve, scan_done, i, j - 1)
                    first = R[:, t % 2, off:off + 1]
                else:
                    first = 1.0
                    before = last_unit[(u, t - 2)] if t >= 2 else last_unit[(1 - u, NT - 2 + t)] - (0 if u else NBODY)
                    unit(dve, a_done, i, before)
                nc.vector.tensor_tensor_scan(R[:, t % 2, off + 1:off + w + 1], z[:, j % 3, 0:w],
                                             zeros[:, 0:w], first, ALU.mult, ALU.max).then_inc(scan_done, 1)

            with dve.Fori(0, ROUNDS) as i:
                for j in range(NBODY + 2):
                    if j < NBODY:
                        scan(i, j)
                    if 0 <= j - 2 < NBODY and not by_act[j - 2]:
                        w = BODY[j - 2][3]
                        unit(dve, t_done, i, j - 2)
                        nc.vector.tensor_copy(aT[:, (j - 2) % 2, 0:w], ps_t[:, (j - 2) % 2, 0:w]) \
                            .then_inc(aT_dve, 1)

        @block.gpsimd
        def _(pool):
            nc.gpsimd.sem_inc(a_done, CR)

            def load_head(i, u):
                half = slice(u * HD, (u + 1) * HD)
                for dst, rows, src, t in (
                        (qs, 0, qk_hi, 0), (qs, HD, qk_lo, 0), (kh, 0, qk_hi, 4), (kh, HD, qk_hi, 4),
                        (kl, 0, qk_lo, 4), (kl, HD, qk_lo, 4)):
                    pool.dma_start(dst[rows:rows + HD, u, :],
                                   src[bass.ds(i + t, 1), half, :].rearrange("a p s -> p (a s)")) \
                        .then_inc(head_in[u], 16)

            load_head(0, 0)
            load_head(0, 1)

            def weights(i, more):
                for j in range(NBODY):
                    _, t, off, w = BODY[j]
                    unit(pool, scan_done, i, j)
                    nc.gpsimd.tensor_tensor(sig[:, j % 4, 0:w], sig[:, j % 4, 0:w],
                                            R[:, t % 2, off:off + w], ALU.mult).then_inc(a_done, 1)
                    if more and (j == NBODY - 1 or BODY[j + 1][0] != BODY[j][0]):
                        load_head(i + 1, BODY[j][0])

            with pool.Fori(0, ROUNDS - 1) as i:
                weights(i, True)
            weights(ROUNDS - 1, False)

        @block.tensor
        def _(pe):
            nc.tensor.sem_inc(z_done, CR)
            nc.tensor.sem_inc(t_done, CR)
            pe.wait_ge(prep, 2)

            def turn_v(i, b):
                if b == 0:
                    pe.wait_ge(v_in, i * 16 + 16)
                else:
                    pe.wait_ge(v_ready, i * 4 + b)
                for t in range(4):
                    last = nc.tensor.transpose(ps_v[:, t * P:(t + 1) * P],
                                               vT[:, (b * 4 + t) * P:(b * 4 + t + 1) * P], ident[:, :])
                last.then_inc(v_turned, 1)

            def scores(i, j):
                u, t, off, w = BODY[j]
                if t == 0 and off == 0:
                    pe.wait_ge(head_in[u], i * 96 + 96)
                unit(pe, scan_done, i, j - 3)
                cols = slice(P * t + off, P * t + off + w)
                q_t = qs[:, u, P * t:P * (t + 1)]
                nc.tensor.matmul(z[:, j % 3, 0:w], q_t, kh[:, u, cols], start=True, stop=False)
                if off == 0:
                    nc.tensor.matmul(z[:, j % 3, 0:P], nident[:, :], mask[:, :], start=False, stop=False)
                nc.tensor.matmul(z[:, j % 3, 0:w], q_t, kl[:, u, cols], start=False, stop=True) \
                    .then_inc(z_done, 1)

            def turn_a(i, j):
                w = BODY[j][3]
                unit(pe, a_done, i, j)
                for b in range(w // P):
                    last = nc.tensor.transpose(ps_t[:, j % 2, b * P:(b + 1) * P],
                                               sig[:, j % 4, b * P:(b + 1) * P], ident[:, :])
                last.then_inc(t_done, 1)

            def product(i, j):
                u, t, off, w = BODY[j]
                if by_act[j]:
                    pe.wait_ge(aT_act, i * sum(by_act) + sum(by_act[:j + 1]))
                else:
                    pe.wait_ge(aT_dve, i * (NBODY - sum(by_act)) + (j + 1 - sum(by_act[:j + 1])))
                group = u * 4 + t // 4
                if off == 0:
                    pe.wait_ge(y_read, i * 8 + (group - 1 + CR))
                if j < 4:
                    pe.wait_ge(v_ready, i * 4 + (j + 1))
                for b in range(w // P):
                    kt = t + off // P + b
                    last = nc.tensor.matmul(ps_y[0:HD, group % 2, (t % 4) * P:(t % 4 + 1) * P],
                                            v[:, kt, u * HD:(u + 1) * HD], aT[:, j % 2, b * P:(b + 1) * P],
                                            start=kt == t, stop=kt == NT - 1)
                if j in ends:
                    last.then_inc(y_done, 1)

            with pe.Fori(0, ROUNDS) as i:
                for j in range(NBODY + 4):
                    if j < 4:
                        turn_v(i, j)
                    if j < NBODY:
                        scores(i, j)
                    if 0 <= j - 3 < NBODY:
                        turn_a(i, j - 3)
                    if j >= 4:
                        product(i, j - 4)


def merge_branches(nc, yaT, ybT, gates, wp_tiles, mT_hi_d, mT_lo_d):
    with ExitStack() as c:
        sb = lambda n, s, d=F32: c.enter_context(nc.sbuf_tensor(n, s, d))
        sem = lambda n: c.enter_context(nc.semaphore(n))
        y_hi = sb("mb_y_hi", [P, 8, S], F32R)
        y_lo = sb("mb_y_lo", [P, 8, S], F32R)
        y = sb("mb_y", [P, 2, 4, TC])
        w = sb("mb_w", [P, 2, KD, P])
        w_hi, w_lo = sb("mb_w_hi", [P, 2, KD, P], F32R), sb("mb_w_lo", [P, 2, KD, P], F32R)
        ga, gb = sb("mb_ga", [P, S]), sb("mb_gb", [P, S])
        ta, tb = sb("mb_ta", [P, TC]), sb("mb_tb", [P, TC])
        m = sb("mb_m", [P, TC])
        m_hi, m_lo = sb("mb_m_hi", [P, 2, TC], F32R), sb("mb_m_lo", [P, 2, TC], F32R)
        ps = c.enter_context(nc.psum_tensor("mb_ps", [P, 4, 2, TC], F32))
        y_in = [sem("mb_y_in0"), sem("mb_y_in1")]
        y_rounded, y_split = sem("mb_y_rounded"), sem("mb_y_split")
        w_in = [sem("mb_w_in0"), sem("mb_w_in1")]
        w_rounded, w_split = sem("mb_w_rounded"), sem("mb_w_split")
        g_in = sem("mb_g_in")
        mm_done = sem("mb_mm_done")
        read_out = sem("mb_read_out")
        dve_step, m_ready = sem("mb_dve_step"), sem("mb_m_ready")
        m_rounded, m_split = sem("mb_m_rounded"), sem("mb_m_split")
        stored = [sem("mb_stored0"), sem("mb_stored1")]
        block = c.enter_context(nc.Block())
        NO = D // P

        @block.gpsimd
        def _(pool):
            for t in range(NC_):
                cols = slice(t * TC, (t + 1) * TC)
                for br, src in enumerate((yaT, ybT)):
                    if t:
                        pool.wait_ge(y_split, 2 * t + br - 1)
                    pool.dma_start(y[:, br, :, :], src[:, :, cols].rearrange("t p s -> p t s")).then_inc(y_in[br], 16)

            def load_gates(n):
                pool.dma_start(ga[:, :], gates[bass.ds(n, 1), :, :].rearrange("a p s -> p (a s)")).then_inc(g_in, 16)
                pool.dma_start(gb[:, :], gates[bass.ds(n + 8, 1), :, :].rearrange("a p s -> p (a s)")).then_inc(g_in, 16)

            load_gates(0)
            with pool.Fori(1, NO) as n:
                pool.wait_ge(read_out, n * NC_ + 4)
                load_gates(n)

        @block.sync
        def _(sp):
            sp.sem_inc(stored[0], 32)
            sp.sem_inc(stored[1], 32)

            def load_w(n, u):
                sp.dma_start(w[:, u, :, :], wp_tiles[bass.ds(n, 1), :, :, :]
                             .rearrange("a p k c -> p (a k) c")).then_inc(w_in[u], 16)

            def store(n, u):
                for t in range(NC_):
                    sp.wait_ge(m_split, n * NC_ + t + 1)
                    for dst, src in ((mT_hi_d, m_hi), (mT_lo_d, m_lo)):
                        sp.dma_start(dst[bass.ds(n, 1), :, t * TC:(t + 1) * TC].rearrange("a p s -> p (a s)"),
                                     src[:, t % 2, :].bitcast(F32)).then_inc(stored[t % 2], 16)

            load_w(0, 0)
            load_w(1, 1)
            with sp.Fori(0, NO // 2 - 1) as i:
                for u in range(2):
                    sp.wait_ge(w_split, i * 2 + u + 3)
                    load_w(i * 2 + u + 2, u)
                    store(i * 2 + u, u)
            for u in range(2):
                store(NO - 2 + u, u)
            for b in range(2):
                sp.wait_ge(stored[b], 32 + NO * NC_ // 2 * 32)

        @block.scalar
        def _(act):
            nc.scalar.sem_inc(w_rounded, 2)

            def round_weight(n, u):
                act.wait_ge(w_in[u], n * 8 - u * 8 + 16)
                act.wait_ge(mm_done, n * NC_ + NC_)
                nc.scalar.copy(w_hi[:, u, :, :], w[:, u, :, :]).then_inc(w_rounded, 1)

            def round_m(n):
                for t in range(NC_):
                    act.wait_ge(m_ready, n * NC_ + t + 1)
                    act.wait_ge(stored[t % 2], n * 64 + t // 2 * 32 + 32)
                    nc.scalar.copy(m_hi[:, t % 2, :], m[:, :]).then_inc(m_rounded, 1)

            round_weight(0, 0)
            round_weight(1, 1)
            for t in range(NC_):
                for br in range(2):
                    act.wait_ge(y_in[br], 16 * (t + 1))
                    nc.scalar.copy(y_hi[:, br * 4:br * 4 + 4, t * TC:(t + 1) * TC], y[:, br, :, :]) \
                        .then_inc(y_rounded, 1)
            with act.Fori(0, NO // 2 - 1) as i:
                for u in range(2):
                    round_m(i * 2 + u)
                    round_weight(i * 2 + u + 2, u)
            for u in range(2):
                round_m(NO - 2 + u)

        @block.vector
        def _(dve):
            nc.vector.sem_inc(w_split, 2)
            nc.vector.sem_inc(read_out, 4)

            def split_weight(n, u):
                dve.wait_ge(w_rounded, n + 3)
                nc.vector.tensor_tensor(w_lo[:, u, :, :], w[:, u, :, :], w_hi[:, u, :, :],
                                        ALU.subtract).then_inc(w_split, 1)

            def gate_chunks(n):
                dve.wait_ge(g_in, n * 32 + 32)
                for t in range(NC_):
                    cols = slice(t * TC, (t + 1) * TC)
                    dve.wait_ge(mm_done, n * NC_ + t + 9)
                    nc.vector.tensor_tensor(ta[:, :], ps[:, t, 0, :], ga[:, cols], ALU.mult).then_inc(dve_step, 1)
                    nc.vector.tensor_tensor(tb[:, :], ps[:, t, 1, :], gb[:, cols], ALU.mult).then_inc(read_out, 1)
                    dve.wait_ge(dve_step, n * NC_ + t + 1)
                    dve.wait_ge(read_out, n * NC_ + t + 5)
                    nc.vector.tensor_tensor(m[:, :], ta[:, :], tb[:, :], ALU.add).then_inc(m_ready, 1)
                    dve.wait_ge(m_rounded, n * NC_ + t + 1)
                    nc.vector.tensor_tensor(m_lo[:, t % 2, :], m[:, :], m_hi[:, t % 2, :],
                                            ALU.subtract).then_inc(m_split, 1)

            split_weight(0, 0)
            split_weight(1, 1)
            for t in range(NC_):
                for br in range(2):
                    dve.wait_ge(y_rounded, 2 * t + br + 1)
                    part = (slice(None), slice(br * 4, br * 4 + 4), slice(t * TC, (t + 1) * TC))
                    nc.vector.tensor_tensor(y_lo[part], y[:, br, :, :], y_hi[part], ALU.subtract).then_inc(y_split, 1)
            with dve.Fori(0, NO // 2 - 1) as i:
                for u in range(2):
                    gate_chunks(i * 2 + u)
                    split_weight(i * 2 + u + 2, u)
            for u in range(2):
                gate_chunks(NO - 2 + u)

        @block.tensor
        def _(pe):
            nc.tensor.sem_inc(mm_done, 8)

            def tile(n, u, wait_y=False):
                pe.wait_ge(w_split, n + 3)
                for t in range(NC_):
                    cols = slice(t * TC, (t + 1) * TC)
                    if wait_y:
                        pe.wait_ge(y_split, 2 * t + 2)
                    pe.wait_ge(read_out, n * NC_ + t + 1)
                    for br in range(2):
                        for k in range(4):
                            kk = br * 4 + k
                            last = passes3(nc, ps[:, t, br, :], w_hi[:, u, kk, :], w_lo[:, u, kk, :],
                                           y_hi[:, kk, cols], y_lo[:, kk, cols], k == 0, k == 3)
                    last.then_inc(mm_done, 1)

            tile(0, 0, True)
            tile(1, 1)
            with pe.Fori(1, NO // 2) as i:
                for u in range(2):
                    tile(i * 2 + u, u)


def output_projection(nc, mT_hi_d, mT_lo_d, wo_d, x, g2, wr_d, ident_d, h2_d, out, logits):
    with ExitStack() as c:
        sb = lambda n, s, d=F32: c.enter_context(nc.sbuf_tensor(n, s, d))
        sem = lambda n: c.enter_context(nc.semaphore(n))
        NR = GR + NE
        wo = sb("op_wo", [P, KD, D])
        wo_hi, wo_lo = sb("op_wo_hi", [P, KD, D], F32R), sb("op_wo_lo", [P, KD, D], F32R)
        m_hi, m_lo = sb("op_m_hi", [P, 2, KD, P], F32R), sb("op_m_lo", [P, 2, KD, P], F32R)
        xt, x1 = sb("op_x", [P, 2, D]), sb("op_x1", [P, 2, D])
        h2, junk = sb("op_h2", [P, 2, D]), sb("op_sq", [P, D])
        h2T = sb("op_h2T", [P, KD, P])
        g_bc, ident = sb("op_g", [P, D]), sb("op_ident", [P, P])
        wr = sb("op_wr", [P, KD, NR])
        eps, ssq = sb("op_eps", [P, 1]), sb("op_ssq", [P, 1])
        rms, rstd = sb("op_rms", [P, 1]), sb("op_rstd", [P, 1])
        ps = c.enter_context(nc.psum_tensor("op_ps", [P, 2, D], F32))
        ps_t = c.enter_context(nc.psum_tensor("op_ps_t", [P, KD, P], F32))
        ps_l = c.enter_context(nc.psum_tensor("op_ps_l", [P, TC], F32))
        const_in = sem("op_const_in")
        wo_in = [sem(f"op_wo_in{k}") for k in range(KD)]
        wo_rounded, wo_split, prep = sem("op_wo_rounded"), sem("op_wo_split"), sem("op_prep")
        tile_in = [sem("op_tile_in0"), sem("op_tile_in1")]
        mm_done, x1_done = sem("op_mm_done"), sem("op_x1_done")
        sq_done, rms_ready, rstd_ready = sem("op_sq_done"), sem("op_rms_ready"), sem("op_rstd_ready")
        h2_ready, turned, h2T_ready = sem("op_h2_ready"), sem("op_turned"), sem("op_h2T_ready")
        l_done, l_read = sem("op_l_done"), sem("op_l_read")
        stored = [sem("op_stored0"), sem("op_stored1")]
        block = c.enter_context(nc.Block())

        @block.gpsimd
        def _(pool):
            nc.gpsimd.memset(eps[:, :], EPS).then_inc(prep, 1)
            def load(n, u):
                cols = bass.ds(n * P, P)
                for dst, src in ((m_hi, mT_hi_d), (m_lo, mT_lo_d)):
                    pool.dma_start(dst[:, u, :, :], src[:, :, cols].rearrange("k p s -> p k s")).then_inc(tile_in[u], 16)
                pool.dma_start(xt[:, u, :], x[cols, :]).then_inc(tile_in[u], 16)

            load(0, 0)
            load(1, 1)
            with pool.Fori(1, NT // 2) as i:
                for u in range(2):
                    pool.wait_ge(x1_done, i * 2 + u + 1)
                    load(i * 2 + u, u)

        @block.sync
        def _(sp):
            for k in range(KD):
                sp.dma_start(wo[:, k, :], wo_d[:, k, :]).then_inc(wo_in[k], 16)
            sp.dma_start(g_bc[:, :], g2.partition_broadcast(P)).then_inc(const_in, 16)
            sp.dma_start(ident[:, :], ident_d).then_inc(const_in, 16)
            sp.dma_start(wr[:, :, :], wr_d).then_inc(const_in, 16)
            sp.sem_inc(stored[0], 32)
            sp.sem_inc(stored[1], 32)
            with sp.Fori(0, NT // 2) as i:
                for u in range(2):
                    rows = bass.ds(i * (2 * P) + u * P, P)
                    sp.wait_ge(x1_done, i * 2 + u + 3)
                    sp.dma_start(out[rows, :], x1[:, u, :]).then_inc(stored[u], 16)
                    sp.wait_ge(h2_ready, i * 2 + u + 1)
                    sp.dma_start(h2_d[rows, :], h2[:, u, :]).then_inc(stored[u], 16)
            sp.dma_start(out[TRASH:OUT_ROWS, :], h2[:, 1, :]).then_inc(stored[1], 16)
            sp.dma_start(h2_d[TRASH:OUT_ROWS, :], h2[:, 1, :]).then_inc(stored[1], 16)
            sp.wait_ge(stored[0], 32 + NT // 2 * 32)
            sp.wait_ge(stored[1], 64 + NT // 2 * 32)

        @block.scalar
        def _(act):
            for k in range(KD):
                act.wait_ge(wo_in[k], 16)
                nc.scalar.copy(wo_hi[:, k, :], wo[:, k, :]).then_inc(wo_rounded, 1)
            act.wait_ge(prep, 1)
            with act.Fori(0, NT) as n:
                act.wait_ge(x1_done, n + 3)
                nc.scalar.activation(junk[:, :], x1[:, bass.ds(n % 2, 1), :]
                                     .rearrange("p a s -> p (a s)"), ACT.Square, accum_out=ssq[:, :]).then_inc(sq_done, 1)
                act.wait_ge(sq_done, n + 1)
                nc.scalar.activation(rms[:, :], ssq[:, :], ACT.Sqrt, scale=1.0 / D, bias=eps[:, :]) \
                    .then_inc(rms_ready, 1)
                act.wait_ge(turned, n + 1)
                nc.scalar.copy(h2T[:, :, :], ps_t[:, :, :]).then_inc(h2T_ready, 1)

        @block.vector
        def _(dve):
            nc.vector.sem_inc(x1_done, 2)
            for k in range(KD):
                dve.wait_ge(wo_rounded, k + 1)
                nc.vector.tensor_tensor(wo_lo[:, k, :], wo[:, k, :], wo_hi[:, k, :],
                                        ALU.subtract).then_inc(wo_split, 1)
            dve.wait_ge(const_in, 48)
            with dve.Fori(0, NT // 2) as i:
                for u in range(2):
                    n = i * 2 + u
                    dve.wait_ge(mm_done, n + 1)
                    dve.wait_ge(stored[u], i * 32 + 32)
                    nc.vector.tensor_tensor(x1[:, u, :], ps[:, u, :], xt[:, u, :], ALU.add).then_inc(x1_done, 1)
                    dve.wait_ge(rms_ready, n + 1)
                    nc.vector.reciprocal(rstd[:, :], rms[:, :]).then_inc(rstd_ready, 1)
                    dve.wait_ge(rstd_ready, n + 1)
                    nc.vector.scalar_tensor_tensor(h2[:, u, :], x1[:, u, :], rstd[:, :], g_bc[:, :],
                                                   ALU.mult, ALU.mult).then_inc(h2_ready, 1)
                    dve.wait_ge(l_done, n + 1)
                    nc.vector.tensor_copy(logits[:, bass.ds(n, 1), :].rearrange("p a e -> p (a e)"),
                                          ps_l[:, 0:NR]).then_inc(l_read, 1)

        @block.tensor
        def _(pe):
            def half(n, u, hf, first=False):
                if hf == 0:
                    pe.wait_ge(tile_in[u], n * 24 - u * 24 + 48)
                    pe.wait_ge(x1_done, n + 1)
                cols = slice(hf * TC, (hf + 1) * TC)
                for k in range(KD):
                    if first:
                        pe.wait_ge(wo_split, k + 1)
                    last = passes3(nc, ps[:, u, cols], m_hi[:, u, k, :],
                                   m_lo[:, u, k, :], wo_hi[:, k, cols],
                                   wo_lo[:, k, cols], k == 0, k == KD - 1)
                if hf:
                    last.then_inc(mm_done, 1)

            def turn(n, u):
                pe.wait_ge(h2_ready, n + 1)
                for k in range(KD):
                    last = nc.tensor.transpose(ps_t[:, k, :], h2[:, u, k * P:(k + 1) * P], ident[:, :])
                last.then_inc(turned, 1)

            def route(n):
                pe.wait_ge(h2T_ready, n + 1)
                if not (isinstance(n, int) and n == 0):
                    pe.wait_ge(l_read, n)
                for k in range(KD):
                    last = nc.tensor.matmul(ps_l[:, 0:NR], h2T[:, k, :], wr[:, k, :], start=k == 0, stop=k == KD - 1)
                last.then_inc(l_done, 1)

            def step(n, u):
                half(n, u, 0)
                turn(n - 1, 1 - u)
                half(n, u, 1)
                route(n - 1)

            half(0, 0, 0, first=True)
            half(0, 0, 1)
            pe.wait_ge(const_in, 48)
            step(1, 1)
            with pe.Fori(1, NT // 2) as i:
                for u in range(2):
                    step(i * 2 + u, u)
            turn(NT - 1, 1)
            route(NT - 1)


C_IOTA, C_REV4, C_REV8, C_THR, C_TOK, C_TRI, C_ONES, C_TRASH = 0, 128, 132, 140, 156, 172, 300, 428
CW = 429
NPC = KD + KF
BT = MAXB + 3


def routing(nc, logits, bias_all, cst_d, w_pieces, idx_all, w_all, blk_tab, wr, w_in):
    with ExitStack() as c:
        sb = lambda n, s, d=F32: c.enter_context(nc.sbuf_tensor(n, s, d))
        sem = lambda n: c.enter_context(nc.semaphore(n))
        NR = GR + NE
        cst = sb("rt_cst", [P, CW])
        b_bc = sb("rt_bias", [P, NR])
        lg = sb("rt_lg", [P, NT, NR])
        gm, gk = sb("rt_gm", [P, NT]), sb("rt_gk", [P, NT])
        gs, key4, ohg = sb("rt_gs", [P, NT, GR]), sb("rt_key4", [P, NT, GR]), sb("rt_ohg", [P, NT, GR])
        gsum, gtop = sb("rt_gsum", [P, NT]), sb("rt_gtop", [P, NT])
        sel, es = sb("rt_sel", [P, NT, GR, EG]), sb("rt_es", [P, NT, EG])
        es2, key8 = sb("rt_es2", [P, NT, EG]), sb("rt_key8", [P, NT, EG])
        oh = [sb("rt_oh0", [P, NT, EG]), sb("rt_oh1", [P, NT, EG])]
        mx = [sb("rt_mx0", [P, NT]), sb("rt_mx1", [P, NT])]
        OH = [sb("rt_OH0", [P, NT, GR, EG]), sb("rt_OH1", [P, NT, GR, EG])]
        O = sb("rt_O", [P, NT, NE])
        acc = sb("rt_acc", [P, NT + 1, NE])
        ed, sd = sb("rt_ed", [P, NT]), sb("rt_sd", [P, NT])
        w = sb("rt_w", [P, 2, NT])
        cmp_, nblk = sb("rt_cmp", [P, NE, NT]), sb("rt_nblk", [P, NE])
        ends, off = sb("rt_ends", [P, NE]), sb("rt_off", [P, NE])
        dest, dsel = sb("rt_dest", [P, NT, NE]), sb("rt_dsel", [P, NT, NE])
        d = sb("rt_d", [P, 2, NT])
        di, hi_i, lo_i = sb("rt_di", [P, 32], I32), sb("rt_hi_i", [P, 32], I32), sb("rt_lo_i", [P, 32], I32)
        hi, lo = sb("rt_hi", [P, 32]), sb("rt_lo", [P, 32])
        row1h = sb("rt_row1h", [P, 2, P])
        blk1h = sb("rt_blk1h", [P, 2, 3, 64])
        tab = sb("rt_tab", [P, 3, 64])
        tmp = sb("rt_tmp", [P, 64])
        ps_r = c.enter_context(nc.psum_tensor("rt_ps_r", [P, NT, NE], F32))
        ps_c = c.enter_context(nc.psum_tensor("rt_ps_c", [P, TC], F32))
        ps_b = c.enter_context(nc.psum_tensor("rt_ps_b", [P, TC], F32))
        const_in, step = sem("rt_const_in"), sem("rt_step")
        exp_in, exp_out = sem("rt_exp_in"), sem("rt_exp_out")
        O_ready, ranks = sem("rt_O_ready"), sem("rt_ranks")
        hot_ready, hot_used = sem("rt_hot_ready"), sem("rt_hot_used")
        block = c.enter_context(nc.Block())
        iota = cst[:, C_IOTA:C_IOTA + P]
        bc = lambda ap, shape: ap.to_broadcast(shape)

        @block.sync
        def _(sp):
            sp.dma_start(cst[:, :], cst_d).then_inc(const_in, 16)
            sp.dma_start(b_bc[:, :], bias_all.partition_broadcast(P)).then_inc(const_in, 16)
            for j in range(NPC):
                sp.dma_start(wr[:, j, :], w_pieces[j, :, :]).then_inc(w_in[j], 16)

        @block.scalar
        def _(act):
            act.wait_ge(exp_in, 1)
            nc.scalar.activation(gs[:, :, :], gs[:, :, :], ACT.Exp).then_inc(exp_out, 1)
            act.wait_ge(exp_in, 2)
            nc.scalar.activation(ed[:, :], ed[:, :], ACT.Exp).then_inc(exp_out, 1)

        @block.tensor
        def _(pe):
            pe.wait_ge(const_in, 32)
            pe.wait_ge(O_ready, 1)
            tri, ones = cst[:, C_TRI:C_TRI + P], cst[:, C_ONES:C_ONES + P]
            nc.tensor.matmul(ps_r[:, :, :], tri, O[:, :, :], start=True, stop=False)
            nc.tensor.matmul(ps_r[:, :, :], ones, acc[:, 0:NT, :], start=False, stop=True)
            nc.tensor.matmul(ps_c[:, 0:NE], ones, acc[:, NT, :], start=True, stop=True).then_inc(ranks, 1)
            for a in range(32):
                pe.wait_ge(hot_ready, a + 1)
                nc.tensor.matmul(ps_b[:, 0:192], row1h[:, a % 2, :],
                                 blk1h[:, a % 2, :, :].rearrange("p c b -> p (c b)"),
                                 start=a == 0, stop=a == 31).then_inc(hot_used, 1)

        @block.vector
        def _(dve):
            V = nc.vector
            ch = Chain(dve, step)
            dve.wait_ge(const_in, 32)
            ch(V.tensor_tensor(lg[:, :, :], logits[:, :, :], bc(b_bc[:, :].unsqueeze(1), [P, NT, NR]), ALU.add))
            G = lg[:, :, 0:GR]
            E = lg[:, :, GR:NR].rearrange("p t (g e) -> p t g e", g=GR)

            def first_max(out1h, src, m, key, kmax, rev, width):
                ch(V.tensor_reduce(m, src, AX.X, ALU.max))
                ch(V.tensor_tensor(key, src, bc(m.unsqueeze(2), [P, NT, width]), ALU.is_equal))
                ch(V.tensor_tensor(key, key, bc(rev.unsqueeze(1), [P, NT, width]), ALU.mult))
                ch(V.tensor_reduce(kmax, key, AX.X, ALU.max))
                ch(V.tensor_tensor(out1h, key, bc(kmax.unsqueeze(2), [P, NT, width]), ALU.is_equal))

            first_max(ohg[:, :, :], G, gm[:, :], key4[:, :, :], gk[:, :], cst[:, C_REV4:C_REV4 + GR], GR)
            V.tensor_tensor(gs[:, :, :], G, bc(gm[:, :].unsqueeze(2), [P, NT, GR]), ALU.subtract).then_inc(exp_in, 1)
            ch(V.tensor_tensor(sel[:, :, :, :], E, bc(ohg[:, :, :].unsqueeze(3), [P, NT, GR, EG]), ALU.mult))
            ch(V.tensor_reduce(es[:, :, :], sel[:, :, :, :].rearrange("p t g e -> p t e g"), AX.X, ALU.add))
            rev8 = cst[:, C_REV8:C_REV8 + EG]
            first_max(oh[0][:, :, :], es[:, :, :], mx[0][:, :], key8[:, :, :], gk[:, :], rev8, EG)
            ch(V.scalar_tensor_tensor(es2[:, :, :], oh[0][:, :, :], -3.0e38, es[:, :, :], ALU.mult, ALU.add))
            first_max(oh[1][:, :, :], es2[:, :, :], mx[1][:, :], key8[:, :, :], gk[:, :], rev8, EG)
            V.tensor_tensor(ed[:, :], mx[1][:, :], mx[0][:, :], ALU.subtract).then_inc(exp_in, 1)
            for k in range(2):
                ch(V.tensor_tensor(OH[k][:, :, :, :], bc(ohg[:, :, :].unsqueeze(3), [P, NT, GR, EG]),
                                   bc(oh[k][:, :, :].unsqueeze(2), [P, NT, GR, EG]), ALU.mult))
            flat = [OH[k][:, :, :, :].rearrange("p t g e -> p t (g e)") for k in range(2)]
            ch(V.tensor_tensor(O[:, :, :], flat[0], flat[1], ALU.add))
            ch(V.memset(acc[:, 0, :], 0.0))
            for t in range(NT):
                ins = V.tensor_tensor(acc[:, t + 1, :], acc[:, t, :], O[:, t, :], ALU.add)
                if t < NT - 1:
                    ch(ins)
            ins.then_inc(O_ready, 1)
            dve.wait_ge(exp_out, 2)
            ch(V.tensor_reduce(gsum[:, :], gs[:, :, :], AX.X, ALU.add))
            ch(V.reciprocal(gtop[:, :], gsum[:, :]))
            ch(V.tensor_scalar(sd[:, :], ed[:, :], 1.0, None, ALU.add))
            ch(V.reciprocal(sd[:, :], sd[:, :]))
            ch(V.tensor_tensor(w[:, 0, :], gtop[:, :], sd[:, :], ALU.mult))
            ch(V.tensor_tensor(w[:, 1, :], w[:, 0, :], ed[:, :], ALU.mult))
            dve.wait_ge(ranks, 1)
            ch(V.tensor_tensor(cmp_[:, :, :], bc(ps_c[:, 0:NE].unsqueeze(2), [P, NE, NT]),
                               bc(cst[:, C_THR:C_THR + NT].unsqueeze(1), [P, NE, NT]), ALU.is_gt))
            ch(V.tensor_reduce(nblk[:, :], cmp_[:, :, :], AX.X, ALU.add))
            ch(V.tensor_tensor_scan(ends[:, :], cst[:, C_ONES:C_ONES + NE], nblk[:, :], 0.0, ALU.mult, ALU.add))
            ch(V.tensor_tensor(off[:, :], ends[:, :], nblk[:, :], ALU.subtract))
            ch(V.tensor_scalar(off[:, :], off[:, :], float(P), None, ALU.mult))
            ch(V.tensor_tensor(dest[:, :, :], ps_r[:, :, :], bc(off[:, :].unsqueeze(1), [P, NT, NE]), ALU.add))
            for k in range(2):
                ch(V.tensor_tensor(dsel[:, :, :], dest[:, :, :], flat[k], ALU.mult))
                ch(V.tensor_reduce(d[:, k, :], dsel[:, :, :], AX.X, ALU.add))
            ch(V.tensor_copy(di[:, :], d[:, :, :].rearrange("p k t -> p (k t)")))
            ch(V.tensor_single_scalar(hi_i[:, :], di[:, :], 7, ALU.logical_shift_right))
            ch(V.tensor_single_scalar(lo_i[:, :], di[:, :], P - 1, ALU.bitwise_and))
            ch(V.tensor_copy(hi[:, :], hi_i[:, :]))
            ch(V.tensor_copy(lo[:, :], lo_i[:, :]))
            for a in range(32):
                k, t = divmod(a, NT)
                if a >= 2:
                    dve.wait_ge(hot_used, a - 1)
                v = a % 2
                V.tensor_scalar(row1h[:, v, :], iota, lo[:, a:a + 1], None, ALU.is_equal)
                V.tensor_scalar(blk1h[:, v, 0, :], iota[:, 0:64], hi[:, a:a + 1], None, ALU.is_equal)
                V.tensor_scalar(blk1h[:, v, 1, :], iota[:, 0:64], hi[:, a:a + 1],
                                cst[:, C_TOK + t:C_TOK + t + 1], ALU.is_equal, ALU.mult)
                V.tensor_scalar(blk1h[:, v, 2, :], iota[:, 0:64], hi[:, a:a + 1], w[:, k, t:t + 1],
                                ALU.is_equal, ALU.mult).then_inc(hot_ready, 1)
            ch(V.tensor_tensor(blk_tab[:, 0:NE], ends[0:1, :], nblk[0:1, :], ALU.subtract))
            ch(V.tensor_copy(blk_tab[:, NE:2 * NE], ends[0:1, :]))
            dve.wait_ge(hot_used, 32)
            ch(V.tensor_copy(tab[:, :, :].rearrange("p c b -> p (c b)"), ps_b[:, 0:192]))
            trash = cst[:, C_TRASH:C_TRASH + 1]
            ch(V.tensor_scalar(tmp[:, :], tab[:, 0, :], trash, None, ALU.mult))
            ch(V.tensor_tensor(tmp[:, :], tab[:, 1, :], tmp[:, :], ALU.subtract))
            ch(V.tensor_scalar(idx_all[:, 1:MAXB + 1], tmp[:, :], trash, None, ALU.add))
            for cols in (slice(0, 1), slice(MAXB + 1, BT)):
                ch(V.tensor_scalar(idx_all[:, cols], iota[:, cols], 0.0, trash, ALU.mult, ALU.add))
            ch(V.memset(w_all[:, 0:1], 0.0))
            ch(V.tensor_copy(w_all[:, 1:MAXB + 1], tab[:, 2, :]))




def experts(nc, h2_d, w_pieces, ident_d, idx_all, w_all, blk_tab, wr, w_in, out):
    with ExitStack() as c:
        sb = lambda n, s, d=F32: c.enter_context(nc.sbuf_tensor(n, s, d))
        sem = lambda n: c.enter_context(nc.semaphore(n))
        HF, HK, QP = F // 2, KF // 2, KD // 2
        DP = NPC - 2
        wh, wl = sb("ex_w_hi", [P, NPC, D], F32R), sb("ex_w_lo", [P, NPC, D], F32R)
        xg = sb("ex_xg", [P, D])
        x_hi, x_lo = sb("ex_x_hi", [P, KD, P], F32R), sb("ex_x_lo", [P, KD, P], F32R)
        s, g = sb("ex_s", [P, 2, HF]), sb("ex_g", [P, 2, HF])
        g_hi, g_lo = sb("ex_g_hi", [P, KF, P], F32R), sb("ex_g_lo", [P, KF, P], F32R)
        y_raw, y = sb("ex_y_raw", [P, D]), sb("ex_y", [P, D])
        w_rows = sb("ex_w_rows", [P, 1])
        ix_x, ix_y = sb("ex_ix_x", [P, 1], I32), sb("ex_ix_y", [P, 1], I32)
        ident = sb("ex_ident", [P, P])
        ps_h = c.enter_context(nc.psum_tensor("ex_ps_h", [P, 2, 2, HF], F32))
        ps_x = c.enter_context(nc.psum_tensor("ex_ps_x", [P, KD, P], F32))
        ps_g = c.enter_context(nc.psum_tensor("ex_ps_g", [P, 2, TC], F32))
        ps_y = c.enter_context(nc.psum_tensor("ex_ps_y", [P, D], F32))
        const_in = sem("ex_const_in")
        w_rounded, w_rounded_pool = sem("ex_w_rounded"), sem("ex_w_rounded_pool")
        w_split, w_split_pool = sem("ex_w_split"), sem("ex_w_split_pool")
        w_used = sem("ex_w_used")
        x_in, x_turned, x_rounded, x_split = (sem("ex_x_" + n) for n in ("in", "turned", "rounded", "split"))
        ix_x_ready, ix_y_ready = sem("ex_ix_x_ready"), sem("ex_ix_y_ready")
        pool_order = sem("ex_pool_order")
        s_ready, dve_step, g_ready = sem("ex_s_ready"), sem("ex_dve_step"), sem("ex_g_ready")
        g_turned, g_rounded, g_split = sem("ex_g_turned"), sem("ex_g_rounded"), sem("ex_g_split")
        y_clear, y_read = sem("ex_y_clear"), sem("ex_y_read")
        y_weighted = sem("ex_y_weighted")
        added = sem("ex_added")
        block = c.enter_context(nc.Block())

        def all_experts(eng, weights, rows):
            def blocks_of(e):
                first = eng.value_load(blk_tab[0:1, bass.ds(e, 1)], min_val=0, max_val=MAXB - 1)
                end = eng.value_load(blk_tab[0:1, bass.ds(e + NE, 1)], min_val=1, max_val=MAXB)
                with eng.Fori(first, end) as b:
                    rows(b, e)
                return end

            weights(0, 0)
            with eng.Fori(0, NE - 1) as e:
                weights(e + 1, blocks_of(e))
            blocks_of(NE - 1)

        def total(eng):
            return eng.value_load(blk_tab[0:1, 2 * NE - 1:2 * NE], min_val=NE, max_val=MAXB)

        @block.sync
        def _(sp):
            sp.dma_start(ident[:, :], ident_d).then_inc(const_in, 16)
            with sp.Fori(1, NE) as e:
                for j in range(NPC):
                    if j < DP:
                        sp.wait_ge(w_split, e * DP + (j + 1))
                    else:
                        sp.wait_ge(w_split_pool, e * 2 + (j - DP + 1))
                    sp.dma_start(wr[:, j, :], w_pieces[bass.ds(e * NPC + j, 1), :, :]
                                 .rearrange("a p c -> p (a c)")).then_inc(w_in[j], 16)

        @block.gpsimd
        def _(pool):
            nc.gpsimd.sem_inc(y_weighted, 1)
            nc.gpsimd.sem_inc(w_split_pool, 2)

            def fetch(b):
                nc.gpsimd.tensor_copy(ix_x[:, :], idx_all[:, bass.ds(b + 1, 1)]).then_inc(ix_x_ready, 1)
                pool.wait_ge(ix_x_ready, b + 1)
                nc.gpsimd.sem_inc(pool_order, 1)
                nc.gpsimd.indirect_dma_start(xg[:, :], None, h2_d,
                                             bass.IndirectOffsetOnAxis(ap=ix_x[:, 0:1], axis=0)) \
                    .then_inc(x_in, 16)

            def add(b):
                nc.gpsimd.tensor_copy(ix_y[:, :], idx_all[:, bass.ds(b, 1)]).then_inc(ix_y_ready, 1)
                nc.gpsimd.tensor_copy(w_rows[:, :], w_all[:, bass.ds(b, 1)]).then_inc(ix_y_ready, 1)
                pool.wait_ge(ix_y_ready, b * 2 + 2)
                pool.wait_ge(y_read, b + 1)
                nc.gpsimd.sem_inc(pool_order, 1)
                nc.gpsimd.tensor_scalar(y[:, :], y_raw[:, :], w_rows[:, :], None, ALU.mult).then_inc(y_weighted, 1)
                pool.wait_ge(y_weighted, b + 2)
                nc.gpsimd.sem_inc(pool_order, 1)
                nc.gpsimd.indirect_dma_start(out, bass.IndirectOffsetOnAxis(ap=ix_y[:, 0:1], axis=0),
                                             y[:, :], None, compute_op=ALU.add).then_inc(added, 16)

            def weights(e, first):
                for j in range(DP, NPC):
                    pool.wait_ge(w_in[j], e * 16 + 16)
                    pool.wait_ge(w_used, first * NPC + (j + 1))
                    nc.gpsimd.sem_inc(pool_order, 1)
                    nc.gpsimd.tensor_copy(wh[:, j, :], wr[:, j, :]).then_inc(w_rounded_pool, 1)
                    pool.wait_ge(w_rounded_pool, e * 2 + (j - DP + 1))
                    nc.gpsimd.tensor_tensor(wl[:, j, :], wr[:, j, :], wh[:, j, :],
                                            ALU.subtract).then_inc(w_split_pool, 1)

            def rows(b, e):
                add(b)
                pool.wait_ge(x_turned, b + 2)
                fetch(b + 2)
                pool.wait_ge(added, b * 16 + 16)

            fetch(0)
            pool.wait_ge(x_turned, 1)
            fetch(1)
            all_experts(pool, weights, rows)
            n = total(pool)
            add(n)
            pool.wait_ge(added, n * 16 + 16)
            pool.wait_ge(x_in, n * 16 + 32)

        @block.scalar
        def _(act):
            def round_x(b):
                act.wait_ge(x_turned, b + 1)
                nc.scalar.copy(x_hi[:, :, :], ps_x[:, :, :]).then_inc(x_rounded, 1)

            def weights(e, first):
                for j in range(DP):
                    act.wait_ge(w_in[j], e * 16 + 16)
                    act.wait_ge(w_used, first * NPC + (j + 1))
                    nc.scalar.copy(wh[:, j, :], wr[:, j, :]).then_inc(w_rounded, 1)

            def rows(b, e):
                def sigmoid(h):
                    act.wait_ge(w_used, b * NPC + (NPC + QP * (h + 1)))
                    nc.scalar.activation(s[:, h, :], ps_h[:, h, 0, :], ACT.Sigmoid).then_inc(s_ready, 1)

                def round_g(h):
                    act.wait_ge(g_turned, b * 2 + (h + 1))
                    nc.scalar.copy(g_hi[:, h * HK:(h + 1) * HK, :].rearrange("p k r -> p (k r)"),
                                   ps_g[:, h, 0:HF]).then_inc(g_rounded, 1)

                sigmoid(0)
                take_y(b)
                sigmoid(1)
                round_g(0)
                round_x(b + 1)
                round_g(1)

            def take_y(b):
                act.wait_ge(w_used, b * NPC + NPC)
                act.wait_ge(y_weighted, b + 1)
                nc.scalar.copy(y_raw[:, :], ps_y[:, :]).then_inc(y_read, 1)

            round_x(0)
            act.wait_ge(y_clear, 1)
            all_experts(act, weights, rows)
            take_y(total(act))

        @block.vector
        def _(dve):
            nc.vector.sem_inc(w_split, DP)
            nc.vector.memset(ps_y[:, :], 0.0).then_inc(y_clear, 1)

            def split_x(b):
                dve.wait_ge(x_rounded, b + 1)
                nc.vector.tensor_tensor(x_lo[:, :, :], ps_x[:, :, :], x_hi[:, :, :], ALU.subtract).then_inc(x_split, 1)

            def weights(e, first):
                for j in range(DP):
                    dve.wait_ge(w_rounded, e * DP + (j + 1))
                    nc.vector.tensor_tensor(wl[:, j, :], wr[:, j, :], wh[:, j, :], ALU.subtract).then_inc(w_split, 1)

            def rows(b, e):
                def silu(h):
                    dve.wait_ge(s_ready, b * 2 + (h + 1))
                    nc.vector.tensor_tensor(s[:, h, :], ps_h[:, h, 0, :], s[:, h, :], ALU.mult).then_inc(dve_step, 1)
                    dve.wait_ge(dve_step, b * 2 + (h + 1))
                    nc.vector.tensor_tensor(g[:, h, :], ps_h[:, h, 1, :], s[:, h, :], ALU.mult).then_inc(g_ready, 1)

                def split_g(h):
                    dve.wait_ge(g_rounded, b * 2 + (h + 1))
                    part = slice(h * HK, (h + 1) * HK)
                    nc.vector.tensor_tensor(g_lo[:, part, :].rearrange("p k r -> p (k r)"), ps_g[:, h, 0:HF],
                                            g_hi[:, part, :].rearrange("p k r -> p (k r)"),
                                            ALU.subtract).then_inc(g_split, 1)

                silu(0)
                silu(1)
                split_g(0)
                split_x(b + 1)
                split_g(1)

            split_x(0)
            all_experts(dve, weights, rows)

        @block.tensor
        def _(pe):
            nc.tensor.sem_inc(w_used, NPC)
            pe.wait_ge(const_in, 16)

            def turn_x(b):
                pe.wait_ge(x_in, b * 16 + 16)
                for k in range(KD):
                    last = nc.tensor.transpose(ps_x[:, k, :], xg[:, k * P:(k + 1) * P], ident[:, :])
                last.then_inc(x_turned, 1)

            def rows(b, e):
                def piece_split(j):
                    if j < DP:
                        pe.wait_ge(w_split, e * DP + (DP + j + 1))
                    else:
                        pe.wait_ge(w_split_pool, e * 2 + (2 + j - DP + 1))

                def up(h):
                    for q in range(QP):
                        j = h * QP + q
                        piece_split(j)
                        for k in (2 * q, 2 * q + 1):
                            cols = slice((k % 2) * F, (k % 2 + 1) * F)
                            last = passes3(nc, ps_h[:, h, :, :].rearrange("p a c -> p (a c)"), x_hi[:, k, :],
                                           x_lo[:, k, :], wh[:, j, cols], wl[:, j, cols], k == 0, k == KD - 1)
                        last.then_inc(w_used, 1)

                def turn_g(h):
                    pe.wait_ge(g_ready, b * 2 + (h + 1))
                    for k in range(HK):
                        last = nc.tensor.transpose(ps_g[:, h, k * P:(k + 1) * P], g[:, h, k * P:(k + 1) * P], ident[:, :])
                    last.then_inc(g_turned, 1)

                def down(k):
                    j = KD + k
                    piece_split(j)
                    for m in range(2):
                        cols = slice(m * TC, (m + 1) * TC)
                        last = passes3(nc, ps_y[:, cols], g_hi[:, k, :], g_lo[:, k, :], wh[:, j, cols], wl[:, j, cols],
                                       k == 0, k == KF - 1)
                    last.then_inc(w_used, 1)

                pe.wait_ge(x_split, b + 1)
                up(0)
                up(1)
                turn_g(0)
                turn_x(b + 1)
                pe.wait_ge(g_split, b * 2 + 1)
                pe.wait_ge(y_read, b + 1)
                down(0)
                turn_g(1)
                down(1)
                pe.wait_ge(g_split, b * 2 + 2)
                down(2)
                down(3)

            turn_x(0)
            all_experts(pe, lambda e, first: None, rows)


def build(nc, x, g1, w_in, b_gate, g_q, g_k, sinks, table, wp, wo, g2, wr, b_all, w_exp,
          ident, pair_ones, neg_ident, mask, onehot, cst, out):
    with ExitStack() as c:
        dram = lambda n, s: nc.dram_tensor(n, s, F32, kind="Internal").ap()
        projF = dram("projF", [NF, P, SPAD])
        qk_hi, qk_lo = dram("qk_hi", [NQK, P, S]), dram("qk_lo", [NQK, P, S])
        gates = dram("gates", [NG, P, S])
        bias_d = dram("band_bias", [8, CHUNK, P])
        yaT, ybT = dram("yaT", [4, P, S]), dram("ybT", [4, P, S])
        mT_hi, mT_lo = dram("mT_hi", [KD, P, S]), dram("mT_lo", [KD, P, S])
        h2 = dram("h2", [OUT_ROWS, D])
        with nc.sbuf_tensor("hT_hi", [P, KD, S], F32R) as hT_hi, nc.sbuf_tensor("hT_lo", [P, KD, S], F32R) as hT_lo:
            norm_transpose(nc, x, g1, ident, hT_hi, hT_lo)
            input_projection(nc, w_in, b_gate, hT_hi, hT_lo, projF, qk_hi, qk_lo, gates)
        band_bias(nc, table, onehot, bias_d)
        banded_attention(nc, projF, g_q, g_k, sinks, bias_d, ident, pair_ones, yaT)
        stick_breaking(nc, projF, qk_hi, qk_lo, ident, neg_ident, mask, ybT)
        merge_branches(nc, yaT, ybT, gates, wp, mT_hi, mT_lo)
        sb = lambda n, s, d: c.enter_context(nc.sbuf_tensor(n, s, d))
        idx_all, w_all = sb("idx_all", [P, BT], I32), sb("w_all", [P, MAXB + 1], F32)
        blk_tab = sb("blk_tab", [1, 2 * NE], I32)
        w_raw = sb("ex_w", [P, NPC, D], F32)
        w_in = [c.enter_context(nc.semaphore(f"ex_w_in{j}")) for j in range(NPC)]
        with nc.sbuf_tensor("logits", [P, NT, GR + NE], F32) as logits:
            output_projection(nc, mT_hi, mT_lo, wo, x, g2, wr, ident, h2, out, logits)
            routing(nc, logits, b_all, cst, w_exp, idx_all, w_all, blk_tab, w_raw, w_in)
        experts(nc, h2, w_exp, ident, idx_all, w_all, blk_tab, w_raw, w_in, out)


def constants():
    f = np.float32
    p = np.arange(P)
    cst = np.zeros((P, CW), f)
    cst[:, C_IOTA:C_IOTA + P] = p
    cst[:, C_REV4:C_REV4 + GR] = np.arange(GR, 0, -1)
    cst[:, C_REV8:C_REV8 + EG] = np.arange(EG, 0, -1)
    cst[:, C_THR:C_THR + NT] = P * np.arange(NT)
    cst[:, C_THR] = -1
    cst[:, C_TOK:C_TOK + NT] = p[:, None] + P * np.arange(NT)
    cst[:, C_TRI:C_TRI + P] = p[:, None] < p[None, :]
    cst[:, C_ONES:C_ONES + P] = 1
    cst[:, C_TRASH] = TRASH + p
    rel = np.arange(CHUNK)[:, None] - np.arange(P)[None, :]
    n = np.abs(rel)
    large = 8 + (np.log(np.maximum(n, 1).astype(f) / f(8)) / f(np.log(16.0)) * f(8)).astype(np.int32)
    bucket = np.where(rel > 0, 16, 0) + np.where(n < 8, n, np.minimum(large, 15))
    onehot = (np.arange(32)[:, None, None] == bucket[None]).astype(f).reshape(32, CHUNK * P)
    return {
        "ident": np.eye(P, dtype=f),
        "pair_ones": np.kron(np.eye(2), np.ones((HD, HD))).astype(f),
        "neg_ident": (-(2.0 ** 100) * np.eye(P)).astype(f),
        "mask": np.tril(np.ones((P, P))).astype(f),
        "onehot": onehot,
        "cst": cst,
    }


def kernel(**inputs):
    import concourse.bacc as bacc
    from concourse.bass_utils import run_bass_kernel_spmd

    a = {k: np.asarray(v) for k, v in inputs.items()}
    w_in = a["w_in"][0]
    aq, akv = 512, 128
    wq = w_in[:, :aq].reshape(D, 2, 4, HD).transpose(0, 2, 1, 3).reshape(D, aq)
    b0 = aq + 2 * akv
    w_cols = np.concatenate([wq, w_in[:, aq:b0], w_in[:, b0 + 1024:b0 + 1536], w_in[:, b0:b0 + 1024],
                             w_in[:, b0 + 1536:]], axis=1)
    wa = a["w_proj_a"][0].reshape(2, 4, HD, D).transpose(1, 0, 2, 3).reshape(512, D)
    wp = np.concatenate([wa, a["w_proj_b"][0]], axis=0)
    rows = lambda w: w.reshape(KD, P, -1).transpose(1, 0, 2)
    tiles = lambda w: w.reshape(KD, P, -1, P).transpose(2, 1, 0, 3)
    w13 = np.stack([a["w1"][0], a["w3"][0]], axis=2).reshape(NE, KD // 2, 2, P, 2, 2, F // 2) \
        .transpose(0, 5, 1, 3, 2, 4, 6).reshape(NE, KD, P, 2 * F)
    w_exp = np.concatenate([w13, a["w2"][0].reshape(NE, KF, P, D)], axis=1).reshape(NE * (KD + KF), P, D)
    arrays = {
        "x": a["x"][0, ::-1],
        "g1": a["norm_mix_g"][0],
        "w_in": tiles(w_cols),
        "b_gate": a["b_gate"][0].reshape(NG, P).T,
        "g_q": a["qa_norm_g"][0].reshape(HD, 1),
        "g_k": a["ka_norm_g"][0].reshape(HD, 1),
        "sinks": a["sinks"][0].reshape(4, 2).T,
        "table": a["rel_bias_table"],
        "wp": tiles(wp),
        "wo": rows(a["w_out"][0]),
        "g2": a["norm_ffn_g"][0],
        "wr": rows(np.concatenate([a["w_group"][0], a["w_router"][0]], axis=1)),
        "b_all": np.concatenate([a["b_group"][0], a["b_router"][0].reshape(-1)]),
        "w_exp": w_exp,
    }
    arrays.update(constants())
    arrays = {k: np.ascontiguousarray(v) for k, v in arrays.items()}
    nc = bacc.Bacc("TRN2", target_bir_lowering=False, num_devices=1)
    aps = {k: nc.dram_tensor("in_" + k, v.shape, mybir.dt.from_np(v.dtype), kind="ExternalInput").ap()
           for k, v in arrays.items()}
    aps["out"] = nc.dram_tensor("out_x", (OUT_ROWS, D), F32, kind="ExternalOutput").ap()
    build(nc, **aps)
    r = run_bass_kernel_spmd(nc, [{"in_" + k: v for k, v in arrays.items()}], core_ids=[0])
    return np.ascontiguousarray(r.results[0]["out_x"][:S][::-1]).reshape(1, S, D)
```
